# Optimizing a Trainium2 kernel written in Bass

```python
import math
import jax
import jax.numpy as jnp
from jax import lax
import numpy as np
import jax, jax.numpy as jnp

D_MODEL = 2048
BATCH = 1
SEQ = 256
DEPTH = 4

N_MIXERS = 4
N_SSD = (DEPTH + 3) // 4
N_FOX = (DEPTH + 2) // 4
N_MLA = (DEPTH + 1) // 4
N_S5 = DEPTH // 4
ALPHA = (2.0 * DEPTH) ** 0.25
BETA = (8.0 * DEPTH) ** -0.25
LN_EPS = 1e-5
RMS_EPS = 1e-6
Q_BLOCK = 128

SSD_EXPAND = 2
SSD_D_INNER = SSD_EXPAND * D_MODEL
SSD_HEADDIM = 64
SSD_HEADS = SSD_D_INNER // SSD_HEADDIM
SSD_GROUPS = 8
SSD_STATE = 128
SSD_CONV = 4
SSD_CHUNK = 128
SSD_CONV_DIM = SSD_D_INNER + 2 * SSD_GROUPS * SSD_STATE
SSD_IN_DIM = SSD_D_INNER + SSD_CONV_DIM + SSD_HEADS
DT_PROJ_SCALE = 0.1

FOX_HEADS = 16
FOX_HEAD_DIM = D_MODEL // FOX_HEADS
FOX_WIDTH = FOX_HEADS * FOX_HEAD_DIM
FOX_IN_DIM = 4 * FOX_WIDTH + FOX_HEADS
FGATE_PROJ_SCALE = 0.1

MLA_HEADS = 16
MLA_Q_RANK = 512
MLA_KV_RANK = 512
MLA_NOPE = 128
MLA_ROPE = 64
MLA_V = 128
MLA_WIDTH = MLA_HEADS * MLA_V
MLA_IN_DIM = MLA_Q_RANK + MLA_KV_RANK + MLA_ROPE + MLA_WIDTH
ROPE_BASE = 10000.0

S5_WIDTH = D_MODEL
S5_GROUP = 16
S5_GROUPS = S5_WIDTH // S5_GROUP
S5_STATE = 64
S5_IN_DIM = 2 * S5_WIDTH


def layer_norm(x, g, b):
    xf = x.astype(jnp.float32)
    mu = jnp.mean(xf, -1, keepdims=True)
    var = jnp.mean(jnp.square(xf - mu), -1, keepdims=True)
    return ((xf - mu) * lax.rsqrt(var + LN_EPS) * g.astype(jnp.float32) + b.astype(jnp.float32)).astype(x.dtype)

def rms_norm(x, w):
    xf = x.astype(jnp.float32)
    y = xf * lax.rsqrt(jnp.mean(jnp.square(xf), -1, keepdims=True) + RMS_EPS)
    return (y * w.astype(jnp.float32)).astype(x.dtype)

def causal_depthwise_conv(x, w, bias):
    k = w.shape[0]
    y = lax.conv_general_dilated(x, w[:, None, :].astype(x.dtype), window_strides=(1,), padding=[(k - 1, 0)], dimension_numbers=('NWC', 'WIO', 'NWC'), feature_group_count=x.shape[-1])
    return y + bias.astype(x.dtype)

def rope_cos_sin(positions, dim):
    inv_freq = ROPE_BASE ** (-jnp.arange(0, dim, 2, dtype=jnp.float32) / dim)
    ang = positions.astype(jnp.float32)[..., None] * inv_freq
    return jnp.cos(ang), jnp.sin(ang)

def apply_rope(x, cos, sin):
    xf = x.astype(jnp.float32)
    x1, x2 = jnp.split(xf, 2, axis=-1)
    return jnp.concatenate([x1 * cos - x2 * sin, x1 * sin + x2 * cos], axis=-1).astype(x.dtype)

def causal_block_attention(q, k, v, scale, cum=None):
    bsz, T, H, dq = q.shape
    nblk = T // Q_BLOCK
    key_pos = jnp.arange(T)
    q_blocks = jnp.moveaxis(q.reshape(bsz, nblk, Q_BLOCK, H, dq), 1, 0)
    starts = jnp.arange(nblk) * Q_BLOCK
    if cum is None:
        xs = (q_blocks, starts)
    else:
        cum = cum.astype(jnp.float32)
        cum_k = jnp.swapaxes(cum, 1, 2)
        xs = (q_blocks, starts, jnp.moveaxis(cum.reshape(bsz, nblk, Q_BLOCK, H), 1, 0))

    def attend(blk):
        qb, s0 = blk[0], blk[1]
        logits = jnp.einsum('bqhd,bkhd->bhqk', qb, k, preferred_element_type=jnp.float32) * scale
        if cum is not None:
            cq = jnp.swapaxes(blk[2], 1, 2)
            logits = logits + cq[..., :, None] - cum_k[:, :, None, :]
        query_pos = s0 + jnp.arange(Q_BLOCK)
        logits = jnp.where(key_pos[None, :] <= query_pos[:, None], logits, -jnp.inf)
        probs = jax.nn.softmax(logits, axis=-1)
        return jnp.einsum('bhqk,bkhd->bqhd', probs.astype(v.dtype), v)

    out = lax.map(attend, xs)
    return jnp.moveaxis(out, 0, 1).reshape(bsz, T, H, v.shape[-1])

def ssd_mixer(h, w_in, conv_w, conv_b, dt_bias, a_log, d_skip, norm_w, w_out):
    bsz, T, _ = h.shape
    G, E, P, N, Q = SSD_GROUPS, SSD_HEADS // SSD_GROUPS, SSD_HEADDIM, SSD_STATE, SSD_CHUNK
    nc = T // Q
    f32 = jnp.float32
    z, xbc, dt = jnp.split(h @ w_in, [SSD_D_INNER, SSD_D_INNER + SSD_CONV_DIM], axis=-1)
    xbc = jax.nn.silu(causal_depthwise_conv(xbc, conv_w, conv_b)).astype(f32)
    xs, bm, cm = jnp.split(xbc, [SSD_D_INNER, SSD_D_INNER + G * N], axis=-1)
    x = xs.reshape(bsz, nc, Q, G, E, P)
    bm = bm.reshape(bsz, nc, Q, G, N)
    cm = cm.reshape(bsz, nc, Q, G, N)
    dt = jax.nn.softplus(dt.astype(f32) + dt_bias.astype(f32)).reshape(bsz, nc, Q, G, E)
    a = -jnp.exp(a_log.astype(f32)).reshape(G, E)
    xdt = x * dt[..., None]
    acs = jnp.moveaxis(jnp.cumsum(dt * a, axis=2), 2, -1)
    idx = jnp.arange(Q)
    seg = acs[..., :, None] - acs[..., None, :]
    decay = jnp.exp(jnp.where(idx[:, None] >= idx[None, :], seg, -jnp.inf))
    cb = jnp.einsum('bclgn,bcsgn->bcgls', cm, bm)
    y_diag = jnp.einsum('bcgls,bcgels,bcsgep->bclgep', cb, decay, xdt)
    decay_to_end = jnp.exp(acs[..., -1:] - acs)
    states = jnp.einsum('bclgn,bcgel,bclgep->bcgepn', bm, decay_to_end, xdt)
    chunk_decay = jnp.exp(acs[..., -1])

    def carry_state(s, inp):
        st, dec = inp
        return s * dec[..., None, None] + st, s

    _, prev = lax.scan(carry_state, jnp.zeros_like(states[:, 0]), (jnp.moveaxis(states, 1, 0), jnp.moveaxis(chunk_decay, 1, 0)))
    prev = jnp.moveaxis(prev, 0, 1)
    y_off = jnp.einsum('bclgn,bcgepn,bcgel->bclgep', cm, prev, jnp.exp(acs))
    y = y_diag + y_off + d_skip.astype(f32).reshape(G, E, 1) * x
    y = y.reshape(bsz, T, SSD_D_INNER) * jax.nn.silu(z.astype(f32))
    yg = y.reshape(bsz, T, G, SSD_D_INNER // G)
    yg = yg * lax.rsqrt(jnp.mean(jnp.square(yg), -1, keepdims=True) + RMS_EPS)
    y = yg.reshape(bsz, T, SSD_D_INNER) * norm_w.astype(f32)
    return y.astype(h.dtype) @ w_out

def fox_mixer(h, w_in, f_bias, w_out):
    bsz, T, _ = h.shape
    W = FOX_WIDTH
    q, k, v, z, f = jnp.split(h @ w_in, [W, 2 * W, 3 * W, 4 * W], axis=-1)
    shp = (bsz, T, FOX_HEADS, FOX_HEAD_DIM)
    log_f = jax.nn.log_sigmoid(f.astype(jnp.float32) + f_bias.astype(jnp.float32))
    cum = jnp.cumsum(log_f, axis=1)
    o = causal_block_attention(q.reshape(shp), k.reshape(shp), v.reshape(shp), FOX_HEAD_DIM ** -0.5, cum)
    y = o.reshape(bsz, T, W) * jax.nn.silu(z)
    return y @ w_out

def mla_mixer(h, positions, w_in, q_norm, kv_norm, w_q_up, w_kv_up, w_out):
    bsz, T, _ = h.shape
    H = MLA_HEADS
    q_lat, kv_lat, k_pe, z = jnp.split(h @ w_in, [MLA_Q_RANK, MLA_Q_RANK + MLA_KV_RANK, MLA_Q_RANK + MLA_KV_RANK + MLA_ROPE], axis=-1)
    q = (rms_norm(q_lat, q_norm) @ w_q_up).reshape(bsz, T, H, MLA_NOPE + MLA_ROPE)
    kv = (rms_norm(kv_lat, kv_norm) @ w_kv_up).reshape(bsz, T, H, MLA_NOPE + MLA_V)
    cos, sin = rope_cos_sin(positions, MLA_ROPE)
    q_pe = apply_rope(q[..., MLA_NOPE:], cos[:, :, None, :], sin[:, :, None, :])
    k_pe = apply_rope(k_pe, cos, sin)
    q = jnp.concatenate([q[..., :MLA_NOPE], q_pe], axis=-1)
    k = jnp.concatenate([kv[..., :MLA_NOPE], jnp.broadcast_to(k_pe[:, :, None, :], (bsz, T, H, MLA_ROPE))], axis=-1)
    o = causal_block_attention(q, k, kv[..., MLA_NOPE:], (MLA_NOPE + MLA_ROPE) ** -0.5)
    y = o.reshape(bsz, T, MLA_WIDTH) * jax.nn.silu(z)
    return y @ w_out

def _diag_linear_combine(left, right):
    a_l, b_l = left
    a_r, b_r = right
    return a_r * a_l, a_r * b_l + b_r

def s5_mixer(h, w_in, lam_re, lam_im, log_step, b_re, b_im, c_re, c_im, d_skip, w_glu, b_glu, w_out):
    bsz, T, _ = h.shape
    f32 = jnp.float32
    u, z = jnp.split(h @ w_in, 2, axis=-1)
    u = u.astype(f32)
    lam = lax.complex(lam_re.astype(f32), lam_im.astype(f32))
    step = jnp.exp(log_step.astype(f32))[:, None]
    lam_bar = jnp.exp(lam * step)
    b_bar = ((lam_bar - 1.0) / lam)[..., None] * lax.complex(b_re.astype(f32), b_im.astype(f32))
    ug = u.reshape(bsz, T, S5_GROUPS, S5_GROUP).astype(jnp.complex64)
    bu = jnp.einsum('gpi,btgi->btgp', b_bar, ug)
    a_seq = jnp.broadcast_to(lam_bar, (1, T, S5_GROUPS, S5_STATE))
    _, states = lax.associative_scan(_diag_linear_combine, (a_seq, bu), axis=1)
    c = lax.complex(c_re.astype(f32), c_im.astype(f32))
    y = jnp.einsum('gip,btgp->btgi', c, states).real.reshape(bsz, T, S5_WIDTH) + d_skip.astype(f32) * u
    y = jax.nn.gelu(y)
    y = y * jax.nn.sigmoid(y @ w_glu.astype(f32) + b_glu.astype(f32))
    y = y * jax.nn.silu(z.astype(f32))
    return y.astype(h.dtype) @ w_out

def _normal(key, shape, std):
    return jax.random.normal(key, shape, jnp.float32) * std

def first_inputs(seed: int = 0) -> dict:
    key = jax.random.key(seed)
    keys = iter(jax.random.split(key, 48))
    D = D_MODEL
    x = _normal(next(keys), (BATCH, SEQ, D), 1.0)
    positions = (jax.random.randint(next(keys), (BATCH, 1), 0, 1024) + jnp.arange(SEQ)[None, :]).astype(jnp.int32)
    ln_g = 1.0 + _normal(next(keys), (DEPTH, D), 0.02)
    ln_b = _normal(next(keys), (DEPTH, D), 0.02)
    L = N_SSD
    ssd_cols = jnp.concatenate([jnp.ones((SSD_IN_DIM - SSD_HEADS,), jnp.float32), jnp.full((SSD_HEADS,), DT_PROJ_SCALE, jnp.float32)])
    ssd_w_in = _normal(next(keys), (L, D, SSD_IN_DIM), D ** -0.5) * ssd_cols
    ssd_conv_w = _normal(next(keys), (L, SSD_CONV, SSD_CONV_DIM), SSD_CONV ** -0.5)
    ssd_conv_b = _normal(next(keys), (L, SSD_CONV_DIM), 0.02)
    dt0 = jnp.exp(jax.random.uniform(next(keys), (L, SSD_HEADS), jnp.float32, math.log(1e-3), math.log(1e-1)))
    ssd_dt_bias = dt0 + jnp.log(-jnp.expm1(-dt0))
    ssd_a_log = jnp.log(jax.random.uniform(next(keys), (L, SSD_HEADS), jnp.float32, 1.0, 16.0))
    ssd_d = 1.0 + _normal(next(keys), (L, SSD_HEADS), 0.1)
    ssd_norm_w = 1.0 + _normal(next(keys), (L, SSD_D_INNER), 0.02)
    ssd_w_out = _normal(next(keys), (L, SSD_D_INNER, D), SSD_D_INNER ** -0.5 * BETA)
    L = N_FOX
    fox_cols = jnp.concatenate([jnp.ones((4 * FOX_WIDTH,), jnp.float32), jnp.full((FOX_HEADS,), FGATE_PROJ_SCALE, jnp.float32)])
    fox_w_in = _normal(next(keys), (L, D, FOX_IN_DIM), D ** -0.5) * fox_cols
    fox_f_bias = jax.random.uniform(next(keys), (L, FOX_HEADS), jnp.float32, 1.0, 6.0)
    fox_w_out = _normal(next(keys), (L, FOX_WIDTH, D), FOX_WIDTH ** -0.5 * BETA)
    L = N_MLA
    mla_w_in = _normal(next(keys), (L, D, MLA_IN_DIM), D ** -0.5)
    mla_q_norm = 1.0 + _normal(next(keys), (L, MLA_Q_RANK), 0.02)
    mla_kv_norm = 1.0 + _normal(next(keys), (L, MLA_KV_RANK), 0.02)
    mla_w_q_up = _normal(next(keys), (L, MLA_Q_RANK, MLA_HEADS * (MLA_NOPE + MLA_ROPE)), MLA_Q_RANK ** -0.5)
    mla_w_kv_up = _normal(next(keys), (L, MLA_KV_RANK, MLA_HEADS * (MLA_NOPE + MLA_V)), MLA_KV_RANK ** -0.5)
    mla_w_out = _normal(next(keys), (L, MLA_WIDTH, D), MLA_WIDTH ** -0.5 * BETA)
    L = N_S5
    s5_w_in = _normal(next(keys), (L, D, S5_IN_DIM), D ** -0.5)
    s5_lambda_re = -0.5 + _normal(next(keys), (L, S5_GROUPS, S5_STATE), 0.01)
    s5_lambda_im = math.pi * jnp.arange(S5_STATE, dtype=jnp.float32) + _normal(next(keys), (L, S5_GROUPS, S5_STATE), 0.01)
    s5_log_step = jax.random.uniform(next(keys), (L, S5_GROUPS), jnp.float32, math.log(1e-3), math.log(1e-1))
    s5_b_re = _normal(next(keys), (L, S5_GROUPS, S5_STATE, S5_GROUP), (2.0 * S5_GROUP) ** -0.5)
    s5_b_im = _normal(next(keys), (L, S5_GROUPS, S5_STATE, S5_GROUP), (2.0 * S5_GROUP) ** -0.5)
    s5_c_re = _normal(next(keys), (L, S5_GROUPS, S5_GROUP, S5_STATE), S5_STATE ** -0.5)
    s5_c_im = _normal(next(keys), (L, S5_GROUPS, S5_GROUP, S5_STATE), S5_STATE ** -0.5)
    s5_d = 1.0 + _normal(next(keys), (L, S5_WIDTH), 0.1)
    s5_w_glu = _normal(next(keys), (L, S5_WIDTH, S5_WIDTH), S5_WIDTH ** -0.5)
    s5_b_glu = _normal(next(keys), (L, S5_WIDTH), 0.02)
    s5_w_out = _normal(next(keys), (L, S5_WIDTH, D), S5_WIDTH ** -0.5 * BETA)
    return {'x': x, 'positions': positions, 'ln_g': ln_g, 'ln_b': ln_b,
            'ssd_w_in': ssd_w_in, 'ssd_conv_w': ssd_conv_w, 'ssd_conv_b': ssd_conv_b, 'ssd_dt_bias': ssd_dt_bias,
            'ssd_a_log': ssd_a_log, 'ssd_d': ssd_d, 'ssd_norm_w': ssd_norm_w, 'ssd_w_out': ssd_w_out,
            'fox_w_in': fox_w_in, 'fox_f_bias': fox_f_bias, 'fox_w_out': fox_w_out,
            'mla_w_in': mla_w_in, 'mla_q_norm': mla_q_norm, 'mla_kv_norm': mla_kv_norm, 'mla_w_q_up': mla_w_q_up,
            'mla_w_kv_up': mla_w_kv_up, 'mla_w_out': mla_w_out,
            's5_w_in': s5_w_in, 's5_lambda_re': s5_lambda_re, 's5_lambda_im': s5_lambda_im, 's5_log_step': s5_log_step,
            's5_b_re': s5_b_re, 's5_b_im': s5_b_im, 's5_c_re': s5_c_re, 's5_c_im': s5_c_im, 's5_d': s5_d,
            's5_w_glu': s5_w_glu, 's5_b_glu': s5_b_glu, 's5_w_out': s5_w_out}

def first_block(x, positions, ln_g, ln_b,
              ssd_w_in, ssd_conv_w, ssd_conv_b, ssd_dt_bias, ssd_a_log, ssd_d, ssd_norm_w, ssd_w_out,
              fox_w_in, fox_f_bias, fox_w_out,
              mla_w_in, mla_q_norm, mla_kv_norm, mla_w_q_up, mla_w_kv_up, mla_w_out,
              s5_w_in, s5_lambda_re, s5_lambda_im, s5_log_step, s5_b_re, s5_b_im, s5_c_re, s5_c_im, s5_d,
              s5_w_glu, s5_b_glu, s5_w_out):
    h = x
    for i in range(DEPTH):
        j = i // N_MIXERS
        kind = i % N_MIXERS
        if kind == 0:
            out = ssd_mixer(h, ssd_w_in[j], ssd_conv_w[j], ssd_conv_b[j], ssd_dt_bias[j], ssd_a_log[j], ssd_d[j], ssd_norm_w[j], ssd_w_out[j])
        elif kind == 1:
            out = fox_mixer(h, fox_w_in[j], fox_f_bias[j], fox_w_out[j])
        elif kind == 2:
            out = mla_mixer(h, positions, mla_w_in[j], mla_q_norm[j], mla_kv_norm[j], mla_w_q_up[j], mla_w_kv_up[j], mla_w_out[j])
        else:
            out = s5_mixer(h, s5_w_in[j], s5_lambda_re[j], s5_lambda_im[j], s5_log_step[j], s5_b_re[j], s5_b_im[j], s5_c_re[j], s5_c_im[j], s5_d[j], s5_w_glu[j], s5_b_glu[j], s5_w_out[j])
        h = layer_norm(ALPHA * h + out.astype(h.dtype), ln_g[i], ln_b[i])
    return h


DEPTH_2 = 1

HEAD_DIM = 128
N_HEADS_DIFF = 6
N_HEADS_MOBA = 4
N_HEADS_DIL = 6
N_SELF_HEADS = N_HEADS_DIFF + N_HEADS_MOBA + N_HEADS_DIL
W_DIFF = N_HEADS_DIFF * HEAD_DIM
W_MOBA = N_HEADS_MOBA * HEAD_DIM
W_DIL = N_HEADS_DIL * HEAD_DIM
MIX_WIDTH = W_DIFF + W_MOBA + W_DIL
DIFF_QK_DIM = HEAD_DIM // 2
MOBA_BLOCK = 256
MOBA_TOPK = 3
MOBA_Q_CHUNK = 64
DIL_PAIRS = ((128, 1), (512, 4), (2048, 16))
DIL_BLOCK = 128
N_BUCKETS = 32
REL_MAX_DIST = 2048
N_MEM = 256
N_MEM_HEADS = 4
MEM_WIDTH = N_MEM_HEADS * HEAD_DIM
D_FF = 5632
CONV_WIDTH = 3
NORM_EPS = 1e-6
NEG_INF = -1e30


def rms_norm_2(x, g):
    xf = x.astype(jnp.float32)
    y = xf * lax.rsqrt(jnp.mean(xf * xf, axis=-1, keepdims=True) + NORM_EPS)
    return (y * g.astype(jnp.float32)).astype(x.dtype)

def t5_bucket(dist):
    n = jnp.maximum(dist, 0)
    max_exact = N_BUCKETS // 2
    nf = jnp.maximum(n, 1).astype(jnp.float32)
    log_ratio = jnp.log(nf / max_exact) / math.log(REL_MAX_DIST / max_exact)
    large = max_exact + (log_ratio * (N_BUCKETS - max_exact)).astype(jnp.int32)
    large = jnp.minimum(large, N_BUCKETS - 1)
    return jnp.where(n < max_exact, n, large)

def rel_bias(table, dist):
    return jnp.moveaxis(table.astype(jnp.float32)[t5_bucket(dist)], -1, 0)

def diff_attention(q, k, v, lam, sub_g, lam_init, table):
    B, S, H, _, dqk = q.shape
    nq = S // Q_BLOCK
    scale = dqk ** -0.5
    qb = q.reshape(B, nq, Q_BLOCK, H, 2, dqk).transpose(1, 0, 3, 4, 2, 5)
    kt = k.transpose(0, 2, 3, 1, 4)
    vt = v.transpose(0, 2, 1, 3)
    kpos = jnp.arange(S)

    def block(args):
        i, qi = args
        qpos = i * Q_BLOCK + jnp.arange(Q_BLOCK)
        dist = qpos[:, None] - kpos[None, :]
        s = jnp.einsum('bhcqd,bhckd->bhcqk', qi, kt).astype(jnp.float32) * scale
        s = s + rel_bias(table, dist)[None, :, None]
        s = jnp.where(dist >= 0, s, NEG_INF)
        p = jax.nn.softmax(s, axis=-1)
        a = p[:, :, 0] - lam * p[:, :, 1]
        return jnp.einsum('bhqk,bhkd->bhqd', a.astype(vt.dtype), vt)

    o = lax.map(block, (jnp.arange(nq), qb))
    o = o.transpose(1, 0, 3, 2, 4).reshape(B, S, H, -1)
    return rms_norm_2(o, sub_g) * (1.0 - lam_init)

def moba_attention(q, k, v, table):
    B, S, H, D = q.shape
    Sp = -(-S // MOBA_BLOCK) * MOBA_BLOCK
    nb = Sp // MOBA_BLOCK
    ksel = min(MOBA_TOPK, nb)
    C = MOBA_Q_CHUNK
    nc = Sp // C
    pad = ((0, 0), (0, Sp - S), (0, 0), (0, 0))
    qt = jnp.pad(q, pad).transpose(0, 2, 1, 3)
    kt = jnp.pad(k, pad).transpose(0, 2, 1, 3)
    vt = jnp.pad(v, pad).transpose(0, 2, 1, 3)
    kb = kt.reshape(B, H, nb, MOBA_BLOCK, D)
    vb = vt.reshape(B, H, nb, MOBA_BLOCK, D)
    kmean = jnp.mean(kb.astype(jnp.float32), axis=3)
    gate = jnp.einsum('bhsd,bhnd->bhsn', qt.astype(jnp.float32), kmean)
    qblk = jnp.arange(Sp) // MOBA_BLOCK
    past = jnp.arange(nb)[None, :] < qblk[:, None]
    gate = jnp.where(past, gate, NEG_INF)
    _, sel = lax.top_k(gate, ksel)
    sel_ok = sel < qblk[:, None]
    qc = qt.reshape(B, H, nc, C, D).transpose(2, 0, 1, 3, 4)
    selc = sel.reshape(B, H, nc, C, ksel).transpose(2, 0, 1, 3, 4)
    okc = sel_ok.reshape(B, H, nc, C, ksel).transpose(2, 0, 1, 3, 4)
    scale = D ** -0.5
    tab_t = table.astype(jnp.float32).T
    bidx = jnp.arange(B)[:, None, None]
    hidx = jnp.arange(H)[None, :, None]
    koff = jnp.arange(MOBA_BLOCK)

    def chunk(args):
        i, qi, si, oki = args
        qpos = i * C + jnp.arange(C)
        own = (i * C) // MOBA_BLOCK
        flat = si.reshape(B, H, C * ksel)
        kg = kb[bidx, hidx, flat].reshape(B, H, C, ksel, MOBA_BLOCK, D)
        vg = vb[bidx, hidx, flat].reshape(B, H, C, ksel, MOBA_BLOCK, D)
        s_sel = jnp.einsum('bhqd,bhqjkd->bhqjk', qi, kg).astype(jnp.float32) * scale
        dist_sel = qpos[None, None, :, None, None] - (si[..., None] * MOBA_BLOCK + koff)
        s_sel = s_sel + tab_t[jnp.arange(H)[None, :, None, None, None], t5_bucket(dist_sel)]
        s_sel = jnp.where(oki[..., None], s_sel, NEG_INF)
        ko = lax.dynamic_slice_in_dim(kt, own * MOBA_BLOCK, MOBA_BLOCK, axis=2)
        vo = lax.dynamic_slice_in_dim(vt, own * MOBA_BLOCK, MOBA_BLOCK, axis=2)
        dist_own = qpos[:, None] - (own * MOBA_BLOCK + koff)[None, :]
        s_own = jnp.einsum('bhqd,bhkd->bhqk', qi, ko).astype(jnp.float32) * scale
        s_own = s_own + rel_bias(table, dist_own)[None]
        s_own = jnp.where(dist_own >= 0, s_own, NEG_INF)
        s = jnp.concatenate([s_sel.reshape(B, H, C, ksel * MOBA_BLOCK), s_own], axis=-1)
        p = jax.nn.softmax(s, axis=-1).astype(vt.dtype)
        p_sel = p[..., :ksel * MOBA_BLOCK].reshape(B, H, C, ksel, MOBA_BLOCK)
        p_own = p[..., ksel * MOBA_BLOCK:]
        return (jnp.einsum('bhqjk,bhqjkd->bhqd', p_sel, vg)
                + jnp.einsum('bhqk,bhkd->bhqd', p_own, vo))

    o = lax.map(chunk, (jnp.arange(nc), qc, selc, okc))
    o = o.transpose(1, 0, 3, 2, 4).reshape(B, Sp, H, D)
    return o[:, :S]

def dilated_branch(q, k, v, table, window, dil):
    B, H, S, D = q.shape
    L = S // dil
    steps = window // dil
    nb = -(-L // DIL_BLOCK)
    Lp = nb * DIL_BLOCK

    def sub(t):
        return t.reshape(B, H, L, dil, D).transpose(0, 1, 3, 2, 4)

    def windowed(t):
        tp = jnp.pad(sub(t), ((0, 0), (0, 0), (0, 0), (DIL_BLOCK, Lp - L), (0, 0)))
        tp = tp.reshape(B, H, dil, nb + 1, DIL_BLOCK, D)
        return jnp.concatenate([tp[:, :, :, :-1], tp[:, :, :, 1:]], axis=4)

    qs = jnp.pad(sub(q), ((0, 0), (0, 0), (0, 0), (0, Lp - L), (0, 0))).reshape(B, H, dil, nb, DIL_BLOCK, D)
    kw = windowed(k)
    vw = windowed(v)
    qi = jnp.arange(DIL_BLOCK)
    ki = jnp.arange(2 * DIL_BLOCK) - DIL_BLOCK
    j = qi[:, None] - ki[None, :]
    kidx = jnp.arange(nb)[:, None, None] * DIL_BLOCK + ki[None, None, :]
    valid = (j >= 0) & (j <= steps) & (kidx >= 0)
    s = jnp.einsum('bhrnqd,bhrnkd->bhrnqk', qs, kw).astype(jnp.float32) * D ** -0.5
    s = s + rel_bias(table, j * dil)[None, :, None, None]
    s = jnp.where(valid, s, NEG_INF)
    lse = jax.nn.logsumexp(s, axis=-1)
    p = jnp.exp(s - lse[..., None]).astype(v.dtype)
    o = jnp.einsum('bhrnqk,bhrnkd->bhrnqd', p, vw)
    o = o.reshape(B, H, dil, Lp, D)[:, :, :, :L].transpose(0, 1, 3, 2, 4).reshape(B, H, S, D)
    lse = lse.reshape(B, H, dil, Lp)[:, :, :, :L].transpose(0, 1, 3, 2).reshape(B, H, S)
    return o, lse

def dilated_attention(q, k, v, table):
    qt, kt, vt = (t.transpose(0, 2, 1, 3) for t in (q, k, v))
    outs, lses = [], []
    for window, dil in DIL_PAIRS:
        o, lse = dilated_branch(qt, kt, vt, table, window, dil)
        outs.append(o)
        lses.append(lse)
    wts = jax.nn.softmax(jnp.stack(lses), axis=0)
    o = jnp.sum(wts[..., None] * jnp.stack(outs).astype(jnp.float32), axis=0)
    return o.astype(q.dtype).transpose(0, 2, 1, 3)

def memory_cross_attention(h, mem_n, w_q, w_kv, w_o):
    B, S, _ = h.shape
    q = (h @ w_q).reshape(B, S, N_MEM_HEADS, HEAD_DIM)
    kv = (mem_n @ w_kv).reshape(B, -1, 2, N_MEM_HEADS, HEAD_DIM)
    k, v = kv[:, :, 0], kv[:, :, 1]
    s = jnp.einsum('bshd,bmhd->bhsm', q, k).astype(jnp.float32) * HEAD_DIM ** -0.5
    p = jax.nn.softmax(s, axis=-1).astype(v.dtype)
    o = jnp.einsum('bhsm,bmhd->bshd', p, v).reshape(B, S, MEM_WIDTH)
    return o @ w_o

def conv_glu_ffn(h, w_up, conv_w, conv_b, w_down):
    gu = h @ w_up
    g, u = jnp.split(gu, 2, axis=-1)
    g = lax.conv_general_dilated(
        g, conv_w[:, None, :].astype(g.dtype), window_strides=(1,),
        padding=[(CONV_WIDTH - 1, 0)], dimension_numbers=('NWC', 'WIO', 'NWC'),
        feature_group_count=D_FF) + conv_b
    return (jax.nn.silu(g) * u) @ w_down

def second_inputs(seed: int = 0) -> dict:
    key = jax.random.key(seed)
    ks = jax.random.split(key, 19)
    f32 = jnp.float32

    def w(k, shape, fan_in):
        return jax.random.normal(k, shape, f32) * fan_in ** -0.5

    def gain(k, shape):
        return 1.0 + 0.02 * jax.random.normal(k, shape, f32)

    return {
        'x': jax.random.normal(ks[0], (BATCH, SEQ, D_MODEL), f32),
        'mem': jax.random.normal(ks[1], (BATCH, N_MEM, D_MODEL), f32),
        'w_in': w(ks[2], (DEPTH_2, D_MODEL, 3 * MIX_WIDTH), D_MODEL),
        'w_out': w(ks[3], (DEPTH_2, MIX_WIDTH, D_MODEL), MIX_WIDTH),
        'g_mix': gain(ks[4], (DEPTH_2, D_MODEL)),
        'diff_lambda': 0.1 * jax.random.normal(ks[5], (DEPTH_2, 4, DIFF_QK_DIM), f32),
        'diff_subln': gain(ks[6], (DEPTH_2, HEAD_DIM)),
        'rel_bias_table': 0.3 * jax.random.normal(ks[7], (N_BUCKETS, N_SELF_HEADS), f32),
        'g_cross': gain(ks[8], (DEPTH_2, D_MODEL)),
        'g_mem': gain(ks[9], (DEPTH_2, D_MODEL)),
        'w_cq': w(ks[10], (DEPTH_2, D_MODEL, MEM_WIDTH), D_MODEL),
        'w_ckv': w(ks[11], (DEPTH_2, D_MODEL, 2 * MEM_WIDTH), D_MODEL),
        'w_co': w(ks[12], (DEPTH_2, MEM_WIDTH, D_MODEL), MEM_WIDTH),
        'g_ffn': gain(ks[13], (DEPTH_2, D_MODEL)),
        'w_up': w(ks[14], (DEPTH_2, D_MODEL, 2 * D_FF), D_MODEL),
        'conv_w': w(ks[15], (DEPTH_2, CONV_WIDTH, D_FF), CONV_WIDTH),
        'conv_b': 0.01 * jax.random.normal(ks[16], (DEPTH_2, D_FF), f32),
        'w_down': w(ks[17], (DEPTH_2, D_FF, D_MODEL), D_FF),
        'g_final': gain(ks[18], (D_MODEL,)),
    }

def second_block(x, mem, w_in, w_out, g_mix, diff_lambda, diff_subln, rel_bias_table,
              g_cross, g_mem, w_cq, w_ckv, w_co, g_ffn, w_up, conv_w, conv_b, w_down, g_final):
    B, S, _ = x.shape
    tab_a = rel_bias_table[:, :N_HEADS_DIFF]
    tab_b = rel_bias_table[:, N_HEADS_DIFF:N_HEADS_DIFF + N_HEADS_MOBA]
    tab_c = rel_bias_table[:, N_HEADS_DIFF + N_HEADS_MOBA:]
    widths = (W_DIFF,) * 3 + (W_MOBA,) * 3 + (W_DIL,) * 3
    cuts = [int(c) for c in np.cumsum(widths)[:-1]]
    for l in range(DEPTH_2):
        h = rms_norm_2(x, g_mix[l])
        qa, ka, va, qb, kb, vb, qc, kc, vc = jnp.split(h @ w_in[l], cuts, axis=-1)
        lam_init = 0.8 - 0.6 * math.exp(-0.3 * l)
        lp = diff_lambda[l].astype(jnp.float32)
        lam = jnp.exp(jnp.sum(lp[0] * lp[1])) - jnp.exp(jnp.sum(lp[2] * lp[3])) + lam_init
        o_a = diff_attention(qa.reshape(B, S, N_HEADS_DIFF, 2, DIFF_QK_DIM),
                             ka.reshape(B, S, N_HEADS_DIFF, 2, DIFF_QK_DIM),
                             va.reshape(B, S, N_HEADS_DIFF, HEAD_DIM),
                             lam, diff_subln[l], lam_init, tab_a)
        o_b = moba_attention(qb.reshape(B, S, N_HEADS_MOBA, HEAD_DIM),
                             kb.reshape(B, S, N_HEADS_MOBA, HEAD_DIM),
                             vb.reshape(B, S, N_HEADS_MOBA, HEAD_DIM), tab_b)
        o_c = dilated_attention(qc.reshape(B, S, N_HEADS_DIL, HEAD_DIM),
                                kc.reshape(B, S, N_HEADS_DIL, HEAD_DIM),
                                vc.reshape(B, S, N_HEADS_DIL, HEAD_DIM), tab_c)
        mixed = jnp.concatenate([o_a.reshape(B, S, W_DIFF), o_b.reshape(B, S, W_MOBA),
                                 o_c.reshape(B, S, W_DIL)], axis=-1)
        x = x + mixed @ w_out[l]
        x = x + memory_cross_attention(rms_norm_2(x, g_cross[l]), rms_norm_2(mem, g_mem[l]),
                                       w_cq[l], w_ckv[l], w_co[l])
        x = x + conv_glu_ffn(rms_norm_2(x, g_ffn[l]), w_up[l], conv_w[l], conv_b[l], w_down[l])
    return rms_norm_2(x, g_final)


def setup_inputs(seed=0):
    out = dict(first_inputs(seed))
    for name, value in second_inputs(seed + 1).items():
        if name != "x":
            out[name + "_2"] = value
    return out


def reference(
    x, positions, ln_g, ln_b, ssd_w_in, ssd_conv_w, ssd_conv_b, ssd_dt_bias, ssd_a_log, ssd_d,
    ssd_norm_w, ssd_w_out, fox_w_in, fox_f_bias, fox_w_out, mla_w_in, mla_q_norm, mla_kv_norm,
    mla_w_q_up, mla_w_kv_up, mla_w_out, s5_w_in, s5_lambda_re, s5_lambda_im, s5_log_step,
    s5_b_re, s5_b_im, s5_c_re, s5_c_im, s5_d, s5_w_glu, s5_b_glu, s5_w_out, mem_2, w_in_2,
    w_out_2, g_mix_2, diff_lambda_2, diff_subln_2, rel_bias_table_2, g_cross_2, g_mem_2, w_cq_2,
    w_ckv_2, w_co_2, g_ffn_2, w_up_2, conv_w_2, conv_b_2, w_down_2, g_final_2,
):
    x = first_block(
        x, positions, ln_g, ln_b, ssd_w_in, ssd_conv_w, ssd_conv_b, ssd_dt_bias, ssd_a_log,
        ssd_d, ssd_norm_w, ssd_w_out, fox_w_in, fox_f_bias, fox_w_out, mla_w_in, mla_q_norm,
        mla_kv_norm, mla_w_q_up, mla_w_kv_up, mla_w_out, s5_w_in, s5_lambda_re, s5_lambda_im,
        s5_log_step, s5_b_re, s5_b_im, s5_c_re, s5_c_im, s5_d, s5_w_glu, s5_b_glu, s5_w_out,
    )
    return second_block(
        x, mem_2, w_in_2, w_out_2, g_mix_2, diff_lambda_2, diff_subln_2, rel_bias_table_2,
        g_cross_2, g_mem_2, w_cq_2, w_ckv_2, w_co_2, g_ffn_2, w_up_2, conv_w_2, conv_b_2,
        w_down_2, g_final_2,
    )


_drawn_inputs = setup_inputs


def setup_inputs(seed=0):
    import zlib

    import numpy as np

    out = dict(_drawn_inputs(seed))
    spreads = {}
    factors = {'ssd_conv_b': 5.59,
     'ssd_norm_w': 8.0,
     'mla_q_norm': 8.0,
     'mla_kv_norm': 8.0,
     's5_lambda_re': 64.0,
     's5_lambda_im': 64.0,
     's5_log_step': 64.0,
     's5_b_re': 64.0,
     's5_b_im': 64.0,
     's5_c_re': 64.0,
     's5_c_im': 64.0,
     's5_d': 6.666,
     's5_w_glu': 2.892,
     's5_b_glu': 8.0,
     'g_mix_2': 3.149,
     'diff_lambda_2': 4.531,
     'diff_subln_2': 5.566,
     'g_cross_2': 8.0,
     'g_mem_2': 8.0,
     'g_ffn_2': 4.094,
     'conv_b_2': 28.654,
     'g_final_2': 7.703}
    for name, (base, spread) in spreads.items():
        noise = np.random.default_rng([zlib.crc32(name.encode()), seed]).standard_normal(out[name].shape)
        drawn = base * np.exp(spread * noise) if base else spread * noise
        out[name] = jnp.asarray(drawn.astype(out[name].dtype))
    for name, factor in factors.items():
        out[name] = (out[name] * factor).astype(out[name].dtype)
    return out
```

```python
from contextlib import ExitStack

import numpy as np

import concourse.bass as bass
from concourse import mybir

F32 = mybir.dt.float32
F32R = mybir.dt.float32r
I32 = mybir.dt.int32
ACT = mybir.ActivationFunctionType
ALU = mybir.AluOpType
AX = mybir.AxisListType

P = 128
T = 256
TT = T // P
D = 2048
KC = D // P
N = 512
SLOT = 4 * N
RAWS = 2
PARTS = 4
LEAD = 3
ALPHA = 8.0 ** 0.25
LN_EPS, RMS_EPS = 1e-5, 1e-6
NEG = -1e30
TWO_PI = 2 * np.pi

SSD_GROUPS, SSD_HEADS, SSD_INNER = 8, 64, 4096
E8 = SSD_HEADS // SSD_GROUPS
FOX_HEADS = MLA_HEADS = MIX_HEADS = 16
DFF = 5632
MEM_HEADS = 4

FOX_SLOT = SSD_GROUPS * 16
MLA_SLOT = FOX_SLOT + 4 * 20
S5_SLOT = MLA_SLOT + 8 + 4 * 12
CKV_SLOT = S5_SLOT + 64
MIX_SLOT = CKV_SLOT + 8
CROSS_SLOT = MIX_SLOT + 8 * 12
FFN_SLOT = CROSS_SLOT + 8
SLOTS = FFN_SLOT + 11 * 12


def weight_stream(w):
    stream = np.zeros((SLOTS, P, SLOT), np.float32)
    at = [0]

    def put(*pieces):
        column = 0
        for m, r, k, c, n in pieces:
            kc = max(x[2] for x in pieces)
            block = m[r:r + k * P, c:c + n].reshape(k, P, n).transpose(1, 0, 2)
            whole = sum(x[4] for x in pieces)
            view = stream[at[0], :, :kc * whole].reshape(P, kc, whole)
            view[:, :, column:column + n] = block
            column += n
        at[0] += 1

    def columns(m, *ranges, rows=D):
        for r in range(0, rows, 4 * P):
            put(*[(m, r, 4, c, n) for c, n in ranges])

    def rows(m, r, k):
        for c in range(0, D, N):
            put((m, r, k, c, N))

    g = w["ssd_w_in"]
    for i in range(SSD_GROUPS + 1):
        if i < SSD_GROUPS:
            columns(g, (8192 + i * P, P), (9216 + i * P, P))
            columns(g, (4096 + i * N, N))
            columns(g, (i * N, N))
        if i:
            rows(w["ssd_w_out"], (i - 1) * N, 4)
    assert at[0] == FOX_SLOT
    for b in range(5):
        for h in range(4 * b, min(4 * b + 4, FOX_HEADS)):
            columns(w["fox_w_in"], *[(i * D + h * P, P) for i in range(4)])
            if b and h == 4 * b + 1:
                rows(w["fox_w_out"], (b - 1) * N, 4)
    rows(w["fox_w_out"], 3 * N, 4)
    assert at[0] == MLA_SLOT
    columns(w["mla_w_in"], (0, N))
    columns(w["mla_w_in"], (N, N))

    def up(h):
        put((w["mla_w_q_up"], 0, 4, h * 192, 192), (w["mla_w_kv_up"], 0, 4, h * T, T))

    for b in range(4):
        up(4 * b)
        for r in range(0, 3):
            put((w["mla_w_in"], r * N, 4, 1088 + b * N, N))
        up(4 * b + 1)
        put((w["mla_w_in"], 3 * N, 4, 1088 + b * N, N))
        if b:
            rows(w["mla_w_out"], (b - 1) * N, 4)
        for h in range(2, 4):
            up(4 * b + h)
    rows(w["mla_w_out"], 3 * N, 4)
    assert at[0] == S5_SLOT
    for j in range(4):
        columns(w["s5_w_in"], (j * N, N))
        columns(w["s5_w_in"], (D + j * N, N))
    for j in range(5):
        if j < 4:
            columns(w["s5_w_glu"], (j * N, N))
        if j:
            rows(w["s5_w_out"], (j - 1) * N, 4)
    assert at[0] == CKV_SLOT
    columns(w["w_ckv_2"], (0, N))
    columns(w["w_ckv_2"], (N, N))
    assert at[0] == MIX_SLOT
    for h in range(MIX_HEADS):
        q, step = mix_columns(h)
        columns(w["w_in_2"], (q, P), (q + step, P), (q + 2 * step, P))
        if h % 2 and h > 1:
            rows(w["w_out_2"], (h // 2 - 1) * T, 2)
    rows(w["w_out_2"], 7 * T, 2)
    assert at[0] == CROSS_SLOT
    columns(w["w_cq_2"], (0, N))
    rows(w["w_co_2"], 0, 4)
    assert at[0] == FFN_SLOT
    for i in range(12):
        if i < 11:
            columns(w["w_up_2"], (i * N, N))
        if i:
            rows(w["w_down_2"], (i - 1) * N, 4)
        if i < 11:
            columns(w["w_up_2"], (DFF + i * N, N))
    assert at[0] == SLOTS
    return stream


def mix_columns(h):
    if h < 6:
        return h * P, 768
    if h < 10:
        return 2304 + (h - 6) * P, 512
    return 3840 + (h - 10) * P, 768


def bucket(dist):
    n = np.maximum(dist, 0)
    ratio = np.log(np.maximum(n, 1).astype(np.float32) / np.float32(16)) / np.float32(np.log(2048 / 16))
    large = np.minimum(16 + (ratio.astype(np.float32) * np.float32(16)).astype(np.int32), 31)
    return np.where(n < 16, n, large)


C_ID, C_TRI, C_TRIQ, C_ONES = 0, 128, 256, 384
C_MASK = 512
C_IOTA = C_MASK + 384
C_PAR = C_IOTA + 256
C_FREQ = C_PAR + 4
C_NHALF = C_FREQ + 32
CONSTS = C_NHALF + 64


def shape_constants():
    c = np.zeros((P, CONSTS), np.float32)
    p = np.arange(P)
    c[:, C_ID:C_ID + P] = np.eye(P)
    c[:, C_TRI:C_TRI + P] = p[:, None] <= p[None, :]
    c[:, C_TRIQ:C_TRIQ + P] = 0.25 * (p[:, None] <= p[None, :])
    c[:, C_ONES:C_ONES + P] = 1
    c[:, C_MASK:C_MASK + P] = np.where(p[None, :] <= p[:, None], 0, NEG)
    k = np.arange(T)
    c[:, C_MASK + P:C_MASK + P + T] = np.where(k[None, :] <= 128 + p[:, None], 0, NEG)
    c[:, C_IOTA:C_IOTA + T] = k
    c[:, C_PAR] = (p // 16) % 2 == 0
    c[:, C_PAR + 1] = (p // 16) % 2 == 1
    c[:, C_PAR + 2] = p < 64
    c[:, C_PAR + 3] = p >= 64
    c[:, C_FREQ:C_FREQ + 32] = np.float32(10000.0) ** (-np.arange(0, 64, 2, dtype=np.float32) / 64)
    c[:, C_NHALF:C_NHALF + 64] = -0.5
    i = np.arange(512)
    dist = 255 - i
    hot = np.zeros((32, 512), np.float32)
    hot[bucket(np.maximum(dist, 0)), i] = 1
    add = np.zeros((16, 512), np.float32)
    add[:10] = np.where(dist >= 0, 0, NEG)
    count = (dist >= 0) * ((dist <= 128) * 1 + (dist % 4 == 0) * 1 + (dist % 16 == 0) * 1)
    add[10:] = np.where(count > 0, np.log(np.maximum(count, 1)), NEG)
    return c, hot, add


def arrays(w):
    w = {k: np.asarray(v) for k, v in w.items()}
    one = {k: v[0] if v.ndim > 1 and v.shape[0] == 1 else v for k, v in w.items()}

    def cols(m):
        return np.ascontiguousarray(m.reshape(-1, P).T)

    def narrow(m, n):
        out = np.zeros((P, KC, 64), np.float32)
        out[:, :, :n] = m.reshape(KC, P, n).transpose(1, 0, 2)
        return out

    con, hot, add = shape_constants()
    taps = np.concatenate([one["ssd_conv_w"], one["ssd_conv_b"][None]]).reshape(5, 48, P).transpose(2, 0, 1)
    ff = np.concatenate([one["conv_w_2"], one["conv_b_2"][None]]).reshape(4, 44, P).transpose(2, 0, 1)
    return {
        "stream": weight_stream(one),
        "x": one["x"],
        "con": con,
        "ssd_rows": np.stack([one["ssd_dt_bias"], one["ssd_a_log"], one["ssd_d"]]),
        "ssd_taps": np.ascontiguousarray(taps),
        "ssd_norm": cols(one["ssd_norm_w"]),
        "ssd_dt": narrow(one["ssd_w_in"][:, 10240:], 64),
        "gains": np.stack([*one["ln_g"][:3], one["g_mem_2"], one["ln_g"][3], one["g_mix_2"], one["g_cross_2"], one["g_ffn_2"],
                           one["g_final_2"]]),
        "ln_b": one["ln_b"],
        "fox_f": narrow(one["fox_w_in"][:, 4 * D:], 16),
        "fox_bias": one["fox_f_bias"][None],
        "mla_kpe": narrow(one["mla_w_in"][:, 1024:1088], 64),
        "lat_w": np.concatenate([one["mla_q_norm"], one["mla_kv_norm"]])[None],
        "positions": np.ascontiguousarray(one["positions"].reshape(TT, P).T),
        "s5_par": np.stack([np.ascontiguousarray(x) for x in (
            one["s5_lambda_re"].reshape(64, P).T, one["s5_lambda_im"].reshape(64, P).T,
            np.repeat(one["s5_log_step"][:, None], 64, 1).reshape(64, P).T)], 1),
        "s5_b": np.stack([one[k].reshape(64, P, 16).transpose(1, 0, 2).reshape(P, 1024)
                          for k in ("s5_b_re", "s5_b_im")], 1).reshape(P, D),
        "s5_c": np.stack([one[k].reshape(KC, P, 64).transpose(1, 0, 2).reshape(P, 1024)
                          for k in ("s5_c_re", "s5_c_im")], 1).reshape(P, D),
        "s5_d": cols(one["s5_d"]),
        "s5_bglu": cols(one["s5_b_glu"]),
        "mem": one["mem_2"],
        "hot": hot,
        "add": add,
        "table": one["rel_bias_table_2"],
        "lambda": one["diff_lambda_2"][None],
        "subln": cols(one["diff_subln_2"]),
        "ff_taps": np.ascontiguousarray(ff),
    }


class At:

    def __init__(self, first, step=0, it=None):
        self.first, self.step, self.it = first, step, it

    def plus(self, k):
        return At(self.first + k, self.step, self.it)

    def half(self):
        assert self.step % 2 == 0
        return At(self.first // 2, self.step // 2, self.it)

    def times(self, k):
        return At(self.first * k, self.step * k, self.it)

    def value(self):
        return self.first if self.it is None else self.it * self.step + self.first


def wait(engine, sem, at, k=0):
    at = at.plus(k) if isinstance(at, At) else At(at + k)
    if at.it is not None:
        assert at.step + at.first > 0
        engine.wait_ge(sem, at.value())
    elif at.first > 0:
        engine.wait_ge(sem, at.first)


class Claims:

    def __init__(self):
        self.used, self.local, self.step, self.it = [0, 0], [0, 0], (0, 0), None

    def loop(self, it, step, start=1):
        self.it, self.step, self.local, self.start = it, step, [0, 0], start

    def end(self, iterations):
        assert self.local == list(self.step), self.local
        self.used = [u + iterations * s for u, s in zip(self.used, self.step)]
        self.loop(None, (0, 0))

    def claim(self, pair):
        if self.it is None:
            self.used[pair] += 1
            return At(self.used[pair] - 1)
        self.local[pair] += 1
        return At(self.used[pair] - self.start * self.step[pair] + self.local[pair] - 1, self.step[pair], self.it)


def build(nc, a):
    with ExitStack() as keep:
        program(nc, a, keep)


def program(nc, a, keep):
    def sb(name, shape, dt=F32, within=keep):
        return within.enter_context(nc.sbuf_tensor(name, shape, dt))

    def sem(name):
        return keep.enter_context(nc.semaphore(name))

    acc = sb("acc", [P, TT, D])
    XH = sb("XH", [P, KC, T], F32R)
    XL = sb("XL", [P, KC, T], F32R)
    raw = sb("raw", [P, RAWS, SLOT])
    WH = sb("WH", [P, PARTS, SLOT], F32R)
    WL = sb("WL", [P, PARTS, SLOT], F32R)
    gain = sb("gain", [P, D])
    offs = sb("offs", [P, D])
    con = sb("con", [P, CONSTS])
    with ExitStack() as s:
        cs5 = sb("cs5", [P, 2, 2, 2, T], within=s)
    with ExitStack() as s:
        rhot = sb("rhot", [32, N], within=s)
        radd = sb("radd", [MIX_HEADS, N], within=s)
        rvec = sb("rvec", [MIX_HEADS, N], within=s)
    YH = sb("YH", [P, 4, T], F32R)
    YL = sb("YL", [P, 4, T], F32R)
    stats = sb("stats", [P, TT, 4, 6])
    mv = sb("mv", [P, TT, 2])
    powin = sb("powin", [P, 4])
    powout = sb("powout", [P, 4])
    small = sb("small", [P, KC, 64])

    ident = con[:, C_ID:C_ID + P]
    tri = con[:, C_TRI:C_TRI + P]
    triq = con[:, C_TRIQ:C_TRIQ + P]
    ones = con[:, C_ONES:C_ONES + P]
    mask = con[:, C_MASK:C_MASK + 384]
    iota = con[:, C_IOTA:C_IOTA + T]

    with ExitStack() as s:
        src = sb("src", [P, TT, D], within=s)
    with ExitStack() as s:
        natbc = sb("natbc", [P, TT, 256], within=s)
        natx = sb("natx", [P, TT, N], within=s)
        natz = sb("natz", [P, TT, N], within=s)
        tz = sb("tz", [P, TT, N], within=s)
        xc = sb("xc", [P, 6, T], within=s)
        em = sb("em", [P, TT, E8, P], within=s)
        decay = sb("decay", [P, 2, 4, P], within=s)
        xdt = sb("xdt", [P, TT, N], within=s)
        dx = natx
        xdte = sb("xdte", [P, N], within=s)
        bnat = sb("bnat", [P, P], within=s)
        cbm = sb("cbm", [P, TT, P], within=s)
        state = sb("state", [P, N], within=s)
        yn = sb("yn", [P, TT, N], within=s)
        dt = sb("dt", [P, TT, 64], within=s)
        dta = sb("dta", [P, TT, 64], within=s)
        dtag = sb("dtag", [P, TT, E8], within=s)
        acsg = sb("acsg", [P, TT, E8], within=s)
        acs = sb("acs", [P, TT, 64], within=s)
        ea = sb("ea", [P, TT, 64], within=s)
        t1, t2, t3 = (yn[:, 0, i * P:i * P + P].rearrange("p (t h) -> p t h", t=TT) for i in range(3))
        cw = sb("cw", [P, 5, 48], within=s)
        cwg = sb("cwg", [P, 5, 6], within=s)
        hrow = sb("hrow", [P, 3, 64], within=s)
        nw = sb("nw", [P, 32], within=s)
        ss = sb("ss", [P, TT], within=s)
    with ExitStack() as s:
        nat = sb("nat", [P, 2, TT, N], within=s)
        qk = sb("qk", [P, 2, T], within=s)
        logit = sb("logit", [P, 384], within=s)
        logit2 = sb("logit2", [P, 384], within=s)
        prob = sb("prob", [P, 512], within=s)
        prob2 = sb("prob2", [P, 384], within=s)
        probT = sb("probT", [P, 512], within=s)
        nmax = sb("nmax", [P, 2, TT], within=s)
        psum_ = sb("psum_", [P, 2, TT], within=s)
        rsum = sb("rsum", [P, 2, TT], within=s)
        yh = sb("yh", [P, TT, P], within=s)
        zz = sb("zz", [P, TT, P], within=s)
        bias = sb("bias", [P, 384], within=s)
        ay = sb("ay", [P, TT], within=s)
        with ExitStack() as s2:
            tzh = sb("tzh", [P, 2, TT, P], within=s2)
            cumk = sb("cumk", [P, FOX_HEADS, T], within=s2)
            lf = sb("lf", [P, TT, 16], within=s2)
            cumq = sb("cumq", [P, TT, 16], within=s2)
            f1 = sb("f1", [P, TT, 16], within=s2)
            f2 = sb("f2", [P, TT, 16], within=s2)
            f3 = sb("f3", [P, TT, 16], within=s2)
            frow = sb("frow", [P, 16], within=s2)
        with ExitStack() as s2:
            lat = sb("lat", [P, 2, TT, N], within=s2)
            LH = sb("LH", [P, 8, T], F32R, within=s2)
            LL = sb("LL", [P, 8, T], F32R, within=s2)
            z4, tz4 = lat[:, 0, :, :], lat[:, 1, :, :]
            latw = sb("latw", [P, 2 * N], within=s2)
            kpe = sb("kpe", [P, TT, 64], within=s2)
            kper = sb("kper", [P, TT, 64], within=s2)
            kpeT = sb("kpeT", [64, T], within=s2)
            qpeT = sb("qpeT", [64, T], within=s2)
            qpe = sb("qpe", [P, TT, 64], within=s2)
            rt = sb("rt", [P, TT, 64], within=s2)
            cossin = sb("cossin", [P, 2, TT, 32], within=s2)
            ang = sb("ang", [P, TT, 32], within=s2)
            angk = sb("angk", [P, TT, 32], within=s2)
            angi = sb("angi", [P, TT], I32, within=s2)
            posf = sb("posf", [P, TT], within=s2)
        with ExitStack() as s2:
            toep = sb("toep", [P, 16, 384], within=s2)
            rtab = sb("rtab", [32, 16], within=s2)
            memk = sb("memk", [P, MEM_HEADS, T], within=s2)
            memv = small[:, :, :].rearrange("p (t c) n -> p t (c n)", t=TT)
            knat = offs[:, 0:2 * N].rearrange("p (t n) -> p t n", t=TT)
            toep_row = toep[:, :, :].rearrange("p h t -> p (h t)")
            cprob = toep_row[:, 0:D].rearrange("p (h q k) -> p h q k", h=MEM_HEADS, q=TT)
            cprobT = toep_row[:, D:2 * D].rearrange("p (h n) -> p h n", h=MEM_HEADS)
            cmax = sb("cmax", [P, MEM_HEADS, TT], within=s2)
            csum = sb("csum", [P, MEM_HEADS, TT], within=s2)
            lrow = sb("lrow", [P, 4, 64], within=s2)
            lprod = sb("lprod", [P, 2, 64], within=s2)
            lam = sb("lam", [P, 4], within=s2)
            subg = sb("subg", [P, 1], within=s2)
    with ExitStack() as s:
        u5 = sb("u5", [P, KC, T], within=s)
        z5 = sb("z5", [P, TT, D], within=s)
        x5 = z5[:, :, 3 * N:4 * N].rearrange("p b (x t) -> p b x t", x=2)
        turns5 = sb("turns5", [P, 2, T], within=s)
        part5 = sb("part5", [P, 2, T], within=s)
        w5 = sb("w5", [P, 2, 4, T], within=s)
        q5 = sb("q5", [P, 4, T], within=s)
        par5 = sb("par5", [P, 3, 64], within=s)
        co5 = sb("co5", [P, 8, 64], within=s)
        d5 = sb("d5", [P, KC], within=s)
        bg5 = sb("bg5", [P, KC], within=s)
        bsel = sb("bsel", [P, 2, 4, 32], within=s)
        csel = sb("csel", [P, 2, 2, 64], within=s)
        wb5 = sb("wb5", [P, 2, P], within=s)
        wc5 = sb("wc5", [P, 9 * P], within=s)
        halfpi = sb("halfpi", [P, 1], within=s)
        uchunk = con[:, C_TRI:C_TRI + T]
        unat = small[:, :, :].rearrange("p (t c) n -> p t (c n)", t=TT)
        b5 = gain[:, :].rearrange("p (c t i) -> p c t i", c=2, i=16)
        c5 = offs[:, :].rearrange("p (c k s) -> p c k s", c=2, s=64)
    with ExitStack() as s:
        natg = sb("natg", [P, TT, N], within=s)
        natu = sb("natu", [P, TT, N], within=s)
        gc = sb("gc", [P, 4, T], within=s)
        tg = sb("tg", [P, 4, T], within=s)
        hh = sb("hh", [P, 4, T], within=s)
        fw = sb("fw", [P, 4, 44], within=s)
        fwg = sb("fwg", [P, 4, 4], within=s)

    bank = [keep.enter_context(nc.psum_tensor(f"bank{i}", [P, N], F32)) for i in range(8)]
    pairs = [(bank[0], bank[1]), (bank[2], bank[3])]
    COPIES = 32
    rvec_dram = nc.dram_tensor("rvec_scratch", [COPIES, MIX_HEADS, N], F32, kind="Internal").ap()

    raw_loaded = [sem(f"raw_loaded{i}") for i in range(RAWS)]
    hi_ready = sem("hi_ready")
    lo_ready = sem("lo_ready")
    slots_used = sem("slots_used")
    free = [sem("pair0_free"), sem("pair1_free")]
    params_loaded = sem("params_loaded")
    x_loaded = sem("x_loaded")
    norm_loaded = sem("norm_loaded")
    src_ready = sem("src_ready")
    xt_done = sem("xt_done")
    xh_ready = sem("xh_ready")
    xl_ready = sem("xl_ready")
    pow_asked = sem("pow_asked")
    pow_done = sem("pow_done")
    act_asked = sem("act_asked")
    act_done = sem("act_done")
    pe_asked = sem("pe_asked")
    pe_done = sem("pe_done")
    nat_ready = sem("nat_ready")
    head_nat = sem("head_nat")
    lat_done = sem("lat_done")
    lath_ready = sem("lath_ready")
    latl_ready = sem("latl_ready")
    cum_read = sem("cum_read")
    small_loaded = sem("small_loaded")
    out_stored = sem("out_stored")
    turned = sem("turned")
    conv_ready = sem("conv_ready")
    tanh_ready = sem("tanh_ready")
    x_silu = sem("x_silu")
    back_done = sem("back_done")
    bnat_ready = sem("bnat_ready")
    xdt_ready = sem("xdt_ready")
    cb_done = sem("cb_done")
    cb_ready = sem("cb_ready")
    acs_done = sem("acs_done")
    seg_ready = sem("seg_ready")
    decay_ready = sem("decay_ready")
    m_ready = sem("m_ready")
    ydiag_done = sem("ydiag_done")
    y_read = sem("y_read")
    state_done = sem("state_done")
    state_ready = sem("state_ready")
    yoff_done = sem("yoff_done")
    gated = sem("gated")
    squared = sem("squared")
    normed = sem("normed")
    yt_done = sem("yt_done")
    yh_ready = sem("yh_ready")
    yl_ready = sem("yl_ready")
    dtag_ready = sem("dtag_ready")
    qkT_done = sem("qkT_done")
    qkT_ready = sem("qkT_ready")
    scores_done = sem("scores_done")
    logits_ready = sem("logits_ready")
    probs_ready = sem("probs_ready")
    mixed_ready = sem("mixed_ready")
    probT_done = sem("probT_done")
    probT_ready = sem("probT_ready")
    pv_done = sem("pv_done")
    head_ready = sem("head_ready")
    headT_done = sem("headT_done")
    headh_ready = sem("headh_ready")
    headl_ready = sem("headl_ready")
    rope_ready = sem("rope_ready")
    rvec_ready = sem("rvec_ready")
    rvec_stored = sem("rvec_stored")
    toep_loaded = sem("toep_loaded")
    s5_loaded = sem("s5_loaded")
    b5_ready = sem("b5_ready")
    co5_ready = sem("co5_ready")
    unat_ready = sem("unat_ready")
    uT_done = sem("uT_done")
    uT_ready = sem("uT_ready")
    sel_ready = sem("sel_ready")
    bcT_done = sem("bcT_done")
    wb_ready = sem("wb_ready")
    wc_ready = sem("wc_ready")
    turns_ready = sem("turns_ready")
    part_ready = sem("part_ready")
    cs_ready = sem("cs_ready")
    bu_done = sem("bu_done")
    bu_read = sem("bu_read")
    scanned = sem("scanned")
    turned_back = sem("turned_back")
    state_made = sem("state_made")
    y5_done = sem("y5_done")
    y5_read = sem("y5_read")
    y5h_ready = sem("y5h_ready")
    y5l_ready = sem("y5l_ready")
    glu_nat = sem("glu_nat")
    ztanh_ready = sem("ztanh_ready")
    zgate_ready = sem("zgate_ready")
    gluT_done = sem("gluT_done")
    gtanh5_ready = sem("gtanh5_ready")
    glu_read = sem("glu_read")
    o5_ready = sem("o5_ready")
    o5h_ready = sem("o5h_ready")
    o5l_ready = sem("o5l_ready")
    gnat_ready = sem("gnat_ready")
    unat2_ready = sem("unat2_ready")
    gT_done = sem("gT_done")
    gconv_ready = sem("gconv_ready")
    gtanh_ready = sem("gtanh_ready")
    uT2_done = sem("uT2_done")
    hidden_ready = sem("hidden_ready")
    fh_ready = sem("fh_ready")
    fl_ready = sem("fl_ready")
    mem_loaded = sem("mem_loaded")
    mix_loaded = sem("mix_loaded")
    bias_done = sem("bias_done")
    kv_nat = sem("kv_nat")
    kT_done = sem("kT_done")
    kT_ready = sem("kT_ready")
    cq_nat = sem("cq_nat")
    cqT_done = sem("cqT_done")
    cqT_ready = sem("cqT_ready")
    cs_done = sem("cs_done")
    cmax_ready = sem("cmax_ready")
    cprob_ready = sem("cprob_ready")
    cpT_done = sem("cpT_done")
    cpT_ready = sem("cpT_ready")
    cpv_done = sem("cpv_done")
    co_nat = sem("co_nat")
    coT_done = sem("coT_done")
    coh_ready = sem("coh_ready")
    col_ready = sem("col_ready")
    fw_loaded = sem("fw_loaded")


    def slot_width(n):
        r = n.first + n.step - MIX_SLOT
        if not 0 <= r < CROSS_SLOT - MIX_SLOT:
            return SLOT
        return 4 * 384 if r < 8 or (r - 8) % 12 < 8 else 2 * N

    def split_high(act, n):
        if n.it is None and n.first >= SLOTS:
            return
        wait(act, raw_loaded[n.first % RAWS], n.half().times(16), 16)
        wait(act, slots_used, n, 1 - PARTS)
        at = slice(0, slot_width(n))
        nc.scalar.activation(WH[:, n.first % PARTS, at], raw[:, n.first % RAWS, at], ACT.Copy).then_inc(hi_ready, 1)

    def split_low(dve, n):
        if n.it is None and n.first >= SLOTS:
            return
        wait(dve, hi_ready, n, 1)
        at = slice(0, slot_width(n))
        nc.vector.tensor_tensor(WL[:, n.first % PARTS, at], raw[:, n.first % RAWS, at],
                                WH[:, n.first % PARTS, at].bitcast(F32), ALU.subtract).then_inc(lo_ready, 1)

    def products(pe, n, chunks, width, pair, first, last, xh=XH, xl=XL, k0=0, cols=None, done=True, only=None):
        wait(pe, lo_ready, n, 1)
        place = n.first % PARTS
        wh = WH[:, place, 0:chunks * width].rearrange("p (k n) -> p k n", k=chunks)
        wl = WL[:, place, 0:chunks * width].rearrange("p (k n) -> p k n", k=chunks)
        lo, hi = cols or (0, width)
        for k in only or range(chunks):
            for tt in range(TT):
                out = pairs[pair][tt][:, lo:hi]
                at = slice(tt * P, tt * P + P)
                start, stop = first and k == 0, last and k == chunks - 1
                nc.tensor.matmul(out, xh[:, k0 + k, at], wh[:, k, lo:hi], start=start, stop=False)
                nc.tensor.matmul(out, xh[:, k0 + k, at], wl[:, k, lo:hi], start=False, stop=False)
                ins = nc.tensor.matmul(out, xl[:, k0 + k, at], wh[:, k, lo:hi], start=False, stop=stop)
        if done:
            ins.then_inc(slots_used, 1)

    def out_products_of(pe, claims, n, c, pair, chunks=4, first=0):
        wait(pe, free[pair], claims.claim(pair))
        products(pe, n.plus(c), chunks, N, pair, True, True, YH, YL, k0=first)

    def add_out(dve, n, c, pair):
        wait(dve, slots_used, n, c + 1)
        for tt in range(TT):
            at = acc[:, tt, c * N:c * N + N]
            ins = nc.vector.tensor_tensor(at, at, pairs[pair][tt][:, :], ALU.add)
        ins.then_inc(free[pair], 1)

    def evacuate(act, dst, pair, n, width=N):
        wait(act, slots_used, n, 1)
        for tt in range(TT):
            ins = nc.scalar.activation(dst[:, tt, 0:width], pairs[pair][tt][:, 0:width], ACT.Copy)
        ins.then_inc(free[pair], 1)

    asked = {"act": 0, "pe": 0, "pow": 0}
    served_pe, served_act, served_pool = [0], [0], [0]

    def ask(kind):
        asked[kind] += 1
        return asked[kind]

    def small_products(pe, out_bank, width):
        for tt in range(TT):
            at = slice(tt * P, tt * P + P)
            for k in range(KC):
                for j, x in enumerate((XH, XL)):
                    ins = nc.tensor.matmul(out_bank[:, tt * width:(tt + 1) * width], x[:, k, at].bitcast(F32),
                                           small[:, k, 0:width], start=k == 0 and j == 0, stop=k == KC - 1 and j == 1)
        return ins


    def turn_tensor(pe, i, source):
        for q in range(8):
            tt, c = q // 4, 4 * (q % 4)
            if i == 0:
                pe.wait_ge(x_loaded, 16)
                pe.wait_ge(params_loaded, 64)
            else:
                pe.wait_ge(src_ready, 4 * turn_after[i] + 2 * tt + c // 8 + 1)
            wait(pe, xl_ready, 8 * i + q - 3)
            for k in range(4):
                ins = nc.tensor.transpose(bank[4 + q % 4][:, k * P:k * P + P],
                                          source[:, tt, (c + k) * P:(c + k + 1) * P], ident)
            ins.then_inc(xt_done, 1)

    def turn_scalar(act, i):
        for q in range(8):
            tt, c = q // 4, 4 * (q % 4)
            act.wait_ge(xt_done, 8 * i + q + 1)
            nc.scalar.activation(XH[:, c:c + 4, tt * P:tt * P + P],
                                 bank[4 + q % 4][:, :].rearrange("p (k t) -> p k t", k=4), ACT.Copy).then_inc(xh_ready, 1)

    def turn_vector(dve, i):
        for q in range(8):
            tt, c = q // 4, 4 * (q % 4)
            dve.wait_ge(xh_ready, 8 * i + q + 1)
            at = (slice(None), slice(c, c + 4), slice(tt * P, tt * P + P))
            nc.vector.tensor_tensor(XL[at], bank[4 + q % 4][:, :].rearrange("p (k t) -> p k t", k=4),
                                    XH[at].bitcast(F32), ALU.subtract).then_inc(xl_ready, 1)

    def scale_residual(dve):
        for tt in range(TT):
            nc.vector.tensor_scalar(acc[:, tt, :], acc[:, tt, :], ALPHA, None, ALU.mult)
        dve.drain()

    turn_after = {0: 0, 1: 0, 2: 1, 3: 2, 4: 3, 5: 5, 6: 6, 7: 7}
    HALVES = [(tt, slice(h * D // 2, (h + 1) * D // 2)) for tt in range(TT) for h in range(2)]

    def statistics(dve, source, c):
        dve.drain()
        for tt in range(TT):
            nc.vector.bn_stats(stats[:, tt, c, :], source[:, tt, c * N:c * N + N])

    def last_out(dve, slot):
        for c in range(4):
            split_low(dve, At(slot + c + LEAD))
            add_out(dve, At(slot), c, c % 2)
            statistics(dve, acc, c)

    def all_statistics(dve):
        dve.drain()
        for tt in range(TT):
            nc.vector.bn_aggr(mv[:, tt, :], stats[:, tt, :, :].rearrange("p c s -> p (c s)"))
        dve.drain()

    def layer_norm_vector(dve, r):
        all_statistics(dve)
        nc.vector.tensor_scalar(powin[:, 0:TT], mv[:, :, 1], LN_EPS, None, ALU.add).then_inc(pow_asked, 1)
        dve.wait_ge(norm_loaded, norm_count[r])
        for i, (tt, at) in enumerate(HALVES):
            nc.vector.scalar_tensor_tensor(acc[:, tt, at], acc[:, tt, at], mv[:, tt, 0:1], gain[:, at],
                                           ALU.subtract, ALU.mult)
            dve.drain()
            if i == 0:
                dve.wait_ge(pow_done, ask("pow"))
            nc.vector.scalar_tensor_tensor(acc[:, tt, at], acc[:, tt, at], powout[:, tt:tt + 1], offs[:, at],
                                           ALU.mult, ALU.add).then_inc(src_ready, 1)

    def rms_norm_vector(dve, r, source, target):
        all_statistics(dve)
        nc.vector.tensor_tensor(powin[:, 0:TT], mv[:, :, 0], mv[:, :, 0], ALU.mult)
        dve.drain()
        nc.vector.scalar_tensor_tensor(powin[:, 0:TT], powin[:, 0:TT], RMS_EPS, mv[:, :, 1], ALU.add,
                                       ALU.add).then_inc(pow_asked, 1)
        dve.wait_ge(norm_loaded, norm_count[r])
        dve.wait_ge(pow_done, ask("pow"))
        for tt, at in HALVES:
            nc.vector.scalar_tensor_tensor(target[:, tt, at], source[:, tt, at], powout[:, tt:tt + 1], gain[:, at],
                                           ALU.mult, ALU.mult).then_inc(src_ready, 1)

    def power(pool, count, width=TT):
        wait(pool, pow_asked, count)
        nc.gpsimd.tensor_tensor(powout[:, 0:width], powin[:, 0:width], con[:, C_NHALF:C_NHALF + width],
                                ALU.pow).then_inc(pow_done, 1)

    LAYER_NORMS = (1, 2, 3, 5)
    norm_count = {}
    loads = 0
    for r in range(1, 10):
        loads += 32 if r in LAYER_NORMS else 16
        norm_count[r] = loads

    def load_norm(pool, r):
        if r > 1:
            pool.wait_ge(src_ready, 4 * (r - 1))
        pool.dma_start(gain[:, :], a["gains"][r - 1, :].partition_broadcast(P)).then_inc(norm_loaded, 16)
        if r in LAYER_NORMS:
            pool.dma_start(offs[:, :], a["ln_b"][LAYER_NORMS.index(r), :].partition_broadcast(P)).then_inc(norm_loaded, 16)


    def ssd_tensor(pe, claims):
        pe.wait_ge(xl_ready, 8)
        pe.wait_ge(small_loaded, 16)
        small_products(pe, bank[4], 64).then_inc(pe_done, 1)
        served_pe[0] += 1
        pe.wait_ge(pe_asked, served_pe[0])
        for c in range(TT):
            nc.tensor.matmul(bank[5][:, c * 64:c * 64 + 64], tri, dta[:, c, :], start=True, stop=True)
        nc.tensor.matmul(bank[5][:, 128:192], ones, dta[:, 0, :], start=True, stop=True).then_inc(pe_done, 1)

        def turn_out(g):
            wait(pe, normed, g, 1)
            for k in range(4):
                for tt in range(TT):
                    ins = nc.tensor.transpose(bank[6 + k // 2][:, (k % 2) * T + tt * P:(k % 2) * T + tt * P + P],
                                              yn[:, tt, k * P:k * P + P], ident)
            ins.then_inc(yt_done, 1)

        def decays(g, k):
            c, half = k // 2, k % 2
            wait(pe, dtag_ready, g, 1)
            if k == 0:
                wait(pe, bnat_ready, g, 1)
            elif k == 1:
                wait(pe, cb_ready, g, 1)
            else:
                wait(pe, seg_ready, g.times(4), k - 1)
            for e in range(4):
                h = half * 4 + e
                ins = nc.tensor.matmul(bank[6 + half][:, e * P:e * P + P],
                                       dtag[:, c, h:h + 1].to_broadcast([P, P]), tri, start=True, stop=True)
            ins.then_inc(acs_done, 1)

        def diagonal(g, c):
            wait(pe, m_ready, g.times(4), 2 * c + 2)
            wait(pe, xdt_ready, g, 1)
            if c == 1:
                wait(pe, state_ready, g, 1)
            for e in range(E8):
                ins = nc.tensor.matmul(bank[4 + c][:, e * 64:e * 64 + 64], em[:, c, e, :],
                                       xdt[:, c, e * 64:e * 64 + 64], start=True, stop=True)
            ins.then_inc(ydiag_done, 1)

        def group(g, n, first):
            wait(pe, free[0], claims.claim(0))
            for s in range(4):
                products(pe, n.plus(s), 4, 256, 0, s == 0, s == 3, k0=4 * s)
            if not first:
                turn_out(g.plus(-1))
            wait(pe, free[1], claims.claim(1))
            for s in range(4):
                products(pe, n.plus(4 + s), 4, N, 1, s == 0, s == 3, k0=4 * s)
            wait(pe, free[0], claims.claim(0))
            products(pe, n.plus(8), 4, N, 0, True, False)
            wait(pe, nat_ready, g.times(2), 1)
            wait(pe, y_read, g.times(3))
            if not first:
                wait(pe, yl_ready, g)
            for k in range(6):
                for tt in range(TT):
                    source = natx[:, tt, k * P:k * P + P] if k < 4 else natbc[:, tt, (k - 4) * P:(k - 3) * P]
                    ins = nc.tensor.transpose(bank[4 + k // 2][:, (k % 2) * T + tt * P:(k % 2) * T + tt * P + P],
                                              source, ident)
            ins.then_inc(turned, 1)
            for s in range(1, 4):
                products(pe, n.plus(8 + s), 4, N, 0, False, s == 3, k0=4 * s)
            wait(pe, x_silu, g, 1)
            for tt in range(TT):
                for k in range(4):
                    nc.tensor.transpose(bank[4 + tt][:, k * P:k * P + P], xc[:, k, tt * P:tt * P + P], ident)
            nc.tensor.transpose(bank[6][:, 0:P], xc[:, 4, 0:P], ident).then_inc(back_done, 1)
            for c in range(TT):
                ins = nc.tensor.matmul(bank[7][:, c * P:c * P + P], xc[:, 4, c * P:c * P + P],
                                       xc[:, 5, c * P:c * P + P], start=True, stop=True)
            ins.then_inc(cb_done, 1)
            decays(g, 0)
            o = n.plus(12)
            if not first:
                out_products_of(pe, claims, o, 0, 1)
            decays(g, 1)
            if not first:
                out_products_of(pe, claims, o, 1, 0)
            decays(g, 2)
            if not first:
                out_products_of(pe, claims, o, 2, 1)
            diagonal(g, 0)
            wait(pe, bnat_ready, g, 1)
            nc.tensor.matmul(bank[5][:, :], bnat[:, :], xdte[:, :], start=True, stop=True).then_inc(state_done, 1)
            decays(g, 3)
            if not first:
                out_products_of(pe, claims, o, 3, 0)
            diagonal(g, 1)
            wait(pe, y_read, g.times(3), 1)
            nc.tensor.matmul(bank[4][:, :], xc[:, 5, P:T], state[:, :], start=True, stop=True).then_inc(yoff_done, 1)

        group(At(0), At(0), True)
        with pe.Fori(1, SSD_GROUPS) as it:
            claims.loop(it, (4, 3))
            group(At(0, 1, it), At(-4, 16, it), False)
            claims.end(SSD_GROUPS - 1)
        turn_out(At(SSD_GROUPS - 1))
        wait(pe, yl_ready, SSD_GROUPS)
        for c in range(4):
            out_products_of(pe, claims, At(FOX_SLOT - 4), c, c % 2)

    def ssd_scalar(act):
        def reply():
            served_act[0] += 1
            act.wait_ge(act_asked, served_act[0])

        reply()
        nc.scalar.activation(t2[:, :, :], t2[:, :, :], ACT.Exp, scale=-1.0)
        nc.scalar.activation(hrow[:, 1, :], hrow[:, 1, :], ACT.Exp)
        act.drain()
        nc.scalar.activation(t3[:, :, :], t2[:, :, :], ACT.Ln, bias=1.0).then_inc(act_done, 1)
        reply()
        nc.scalar.activation(ea[:, :, :], ea[:, :, :], ACT.Exp).then_inc(act_done, 1)

        def high_out(g):
            wait(act, yt_done, g, 1)
            for k in range(4):
                ins = nc.scalar.activation(YH[:, k, :], bank[6 + k // 2][:, (k % 2) * T:(k % 2) * T + T], ACT.Copy,
                                           scale=nwg(g, k))
            ins.then_inc(yh_ready, 1)

        def exps(g, k):
            wait(act, seg_ready, g.times(4), k + 1)
            nc.scalar.activation(decay[:, k % 2, :, :], decay[:, k % 2, :, :], ACT.Exp).then_inc(decay_ready, 1)

        def group(g, n, first):
            for s in range(4):
                split_high(act, n.plus(s + LEAD))
            wait(act, gated, g)
            evacuate(act, natbc, 0, n.plus(3), 256)
            if not first:
                high_out(g.plus(-1))
            for s in range(4, 8):
                split_high(act, n.plus(s + LEAD))
            evacuate(act, natx, 1, n.plus(7))
            act.drain().then_inc(nat_ready, 1)
            for s in range(8, 10):
                split_high(act, n.plus(s + LEAD))
            wait(act, conv_ready, g, 1)
            wait(act, ydiag_done, g.times(2))
            nc.scalar.activation(em[:, :, :, :].rearrange("p c e t -> p (c e t)")[:, 0:6 * T],
                                 xc[:, :, :].rearrange("p k t -> p (k t)"), ACT.Tanh, scale=0.5).then_inc(tanh_ready, 1)
            split_high(act, n.plus(10 + LEAD))
            wait(act, back_done, g, 1)
            wait(act, state_done, g)
            nc.scalar.activation(bnat[:, :], bank[6][:, 0:P], ACT.Copy).then_inc(bnat_ready, 1)
            split_high(act, n.plus(11 + LEAD))
            wait(act, normed, g)
            evacuate(act, natz, 0, n.plus(11))
            exps(g, 0)
            if not first:
                split_high(act, n.plus(12 + LEAD))
            act.drain()
            nc.scalar.activation(tz[:, :, :], natz[:, :, :], ACT.Tanh, scale=0.5).then_inc(nat_ready, 1)
            exps(g, 1)
            if not first:
                split_high(act, n.plus(13 + LEAD))
            exps(g, 2)
            if not first:
                split_high(act, n.plus(14 + LEAD))
            wait(act, state_done, g, 1)
            wait(act, yoff_done, g)
            nc.scalar.activation(state[:, :], bank[5][:, :], ACT.Copy, scale=0.25).then_inc(state_ready, 1)
            exps(g, 3)
            if not first:
                split_high(act, n.plus(15 + LEAD))
            wait(act, gated, g, 1)
            for tt in range(TT):
                ins = nc.scalar.activation(tz[:, tt, :], yn[:, tt, :], ACT.Square, accum_out=ss[:, tt:tt + 1])
            act.drain().then_inc(squared, 1)

        group(At(0), At(0), True)
        with act.Fori(1, SSD_GROUPS) as it:
            group(At(0, 1, it), At(-4, 16, it), False)
        wait(act, slots_used, FOX_SLOT - 4)
        high_out(At(SSD_GROUPS - 1))
        for c in range(4):
            split_high(act, At(FOX_SLOT - 4 + c + LEAD))

    def nwg(g, k):
        if g.it is None:
            return nw[:, 4 * g.first + k:4 * g.first + k + 1]
        return nw[:, bass.ds(g.it * 4 + (4 * g.first + k), 1)]

    def ssd_vector(dve):
        dve.wait_ge(params_loaded, 16 * 4)
        dve.wait_ge(pe_done, 1)
        b4 = bank[4][:, 0:128].rearrange("p (t h) -> p t h", t=TT)
        nc.vector.tensor_tensor(t1[:, :, :], b4, hrow[:, 0:1, :].to_broadcast([P, TT, 64]), ALU.add)
        dve.drain()
        nc.vector.scalar_tensor_tensor(t2[:, :, :], t1[:, :, :], -1.0, t1[:, :, :], ALU.mult, ALU.max).then_inc(act_asked, 1)
        dve.wait_ge(act_done, ask("act"))
        nc.vector.tensor_scalar(acs[:, :, :], t2[:, :, :], 1.0, None, ALU.add)
        dve.drain()
        nc.vector.reciprocal(dta[:, :, :], acs[:, :, :])
        nc.vector.scalar_tensor_tensor(acs[:, :, :], acs[:, :, :], -1.0, t2[:, :, :], ALU.add, ALU.subtract)
        dve.drain()
        nc.vector.tensor_tensor(acs[:, :, :], acs[:, :, :], dta[:, :, :], ALU.mult)
        dve.drain()
        nc.vector.tensor_tensor(t3[:, :, :], t3[:, :, :], acs[:, :, :], ALU.subtract)
        dve.drain()
        nc.vector.scalar_tensor_tensor(t1[:, :, :], t1[:, :, :], 0.0, t3[:, :, :], ALU.max, ALU.add)
        dve.drain()
        nc.vector.tensor_scalar(dt[:, :, :], t1[:, :, :], 0.5, None, ALU.mult)
        for tt in range(TT):
            ins = nc.vector.scalar_tensor_tensor(dta[:, tt, :], t1[:, tt, :], -1.0, hrow[:, 1, :], ALU.mult, ALU.mult)
        ins.then_inc(pe_asked, 1)
        ask("pe")
        nc.vector.tensor_scalar(hrow[:, 2, :], hrow[:, 2, :], 0.5, None, ALU.mult)
        dve.wait_ge(pe_done, 2)
        nc.vector.tensor_copy(acs[:, :, :].rearrange("p t h -> p (t h)"), bank[5][:, 0:128])
        dve.drain()
        nc.vector.tensor_tensor(ea[:, 0, :], bank[5][:, 128:192], acs[:, 0, :], ALU.subtract)
        nc.vector.tensor_copy(ea[:, 1, :], acs[:, 1, :]).then_inc(act_asked, 1)
        dve.wait_ge(act_done, ask("act"))

        def heads(x, g, lo=0, n=E8):
            if g.it is None:
                return x[:, g.first * E8 + lo:g.first * E8 + lo + n]
            return x[:, bass.ds(g.it * E8 + (g.first * E8 + lo), n)]

        def wide(x):
            return x.unsqueeze(2).to_broadcast([P, E8, 64])

        def by_head(x):
            return x.rearrange("p (e c) -> p e c", c=64)

        def low_out(g):
            wait(dve, yh_ready, g, 1)
            for k in range(4):
                ins = nc.vector.scalar_tensor_tensor(
                    YL[:, k, :], bank[6 + k // 2][:, (k % 2) * T:(k % 2) * T + T], nwg(g, k),
                    YH[:, k, :].bitcast(F32), ALU.mult, ALU.subtract)
            ins.then_inc(yl_ready, 1)

        def seg(g, k):
            c, half = k // 2, k % 2
            dve.drain()
            wait(dve, acs_done, g.times(4), k + 1)
            for e in range(4):
                h = 4 * half + e
                ins = nc.vector.tensor_scalar(decay[:, k % 2, e, :], bank[6 + half][:, e * P:e * P + P],
                                              acsg[:, c, h:h + 1], 0.0, ALU.subtract, ALU.min)
            ins.then_inc(seg_ready, 1)

        def weighted(g, k):
            c, half = k // 2, k % 2
            wait(dve, decay_ready, g.times(4), k + 1)
            nc.vector.tensor_tensor(em[:, c, 4 * half:4 * half + 4, :], decay[:, k % 2, :, :],
                                    cbm[:, c:c + 1, :].to_broadcast([P, 4, P]), ALU.mult).then_inc(m_ready, 1)

        def group(g, n, first):
            for s in range(4):
                split_low(dve, n.plus(s + LEAD))
            if not first:
                low_out(g.plus(-1))
            if g.it is None:
                xs = slice(4 * g.first, 4 * g.first + 4)
                bc = slice(32 + g.first, 48, 8)
                nc.vector.tensor_copy(cwg[:, :, 4:6], cw[:, :, bc])
            else:
                xs = bass.ds(g.it * 4, 4)
                for j in range(2):
                    nc.vector.tensor_copy(cwg[:, :, 4 + j:5 + j], cw[:, :, bass.ds(g.it + (32 + 8 * j), 1)])
            nc.vector.tensor_copy(cwg[:, :, 0:4], cw[:, :, xs])
            for c in range(TT):
                nc.vector.tensor_copy(acsg[:, c, :], heads(acs[:, c, :], g))
                ins = nc.vector.tensor_copy(dtag[:, c, :], heads(dta[:, c, :], g))
            ins.then_inc(dtag_ready, 1)
            for s in range(4, 8):
                split_low(dve, n.plus(s + LEAD))
            wait(dve, turned, g, 1)
            for j in range(4):
                for k in range(6):
                    b = bank[4 + k // 2][:, (k % 2) * T:(k % 2) * T + T]
                    if j == 0:
                        ins = nc.vector.tensor_scalar(xc[:, k, :], b, cwg[:, 3, k:k + 1], cwg[:, 4, k:k + 1],
                                                      ALU.mult, ALU.add)
                    else:
                        ins = nc.vector.scalar_tensor_tensor(xc[:, k, j:T], b[:, 0:T - j], cwg[:, 3 - j, k:k + 1],
                                                             xc[:, k, j:T], ALU.mult, ALU.add)
                if j == 1:
                    split_low(dve, n.plus(8 + LEAD))
                if j < 3:
                    dve.drain()
            ins.then_inc(conv_ready, 1)
            split_low(dve, n.plus(9 + LEAD))
            wait(dve, tanh_ready, g, 1)
            flat = xc[:, :, :].rearrange("p k t -> p (k t)")
            nc.vector.scalar_tensor_tensor(flat, em[:, :, :, :].rearrange("p c e t -> p (c e t)")[:, 0:6 * T], 1.0,
                                           flat, ALU.add, ALU.mult).then_inc(x_silu, 1)
            split_low(dve, n.plus(10 + LEAD))
            wait(dve, back_done, g, 1)
            for tt in range(TT):
                nc.vector.tensor_tensor(by_head(xdt[:, tt, :]), by_head(bank[4 + tt][:, :]),
                                        wide(heads(dt[:, tt, :], g)), ALU.mult)
                nc.vector.tensor_tensor(by_head(dx[:, tt, :]), by_head(bank[4 + tt][:, :]),
                                        wide(heads(hrow[:, 2, :], g)), ALU.mult)
            dve.drain()
            nc.vector.tensor_tensor(by_head(xdte[:, :]), by_head(xdt[:, 0, :]), wide(heads(ea[:, 0, :], g)),
                                    ALU.mult).then_inc(xdt_ready, 1)
            wait(dve, cb_done, g, 1)
            nc.vector.tensor_tensor(cbm[:, :, :], bank[7][:, 0:T].rearrange("p (c t) -> p c t", c=TT),
                                    triq.unsqueeze(1).to_broadcast([P, TT, P]), ALU.mult).then_inc(cb_ready, 1)
            seg(g, 0)
            split_low(dve, n.plus(11 + LEAD))
            weighted(g, 0)
            o = n.plus(12)
            if not first:
                split_low(dve, n.plus(12 + LEAD))
            seg(g, 1)
            if not first:
                add_out(dve, o, 0, 1)
            weighted(g, 1)
            if not first:
                split_low(dve, n.plus(13 + LEAD))
            seg(g, 2)
            if not first:
                add_out(dve, o, 1, 0)
            weighted(g, 2)
            if not first:
                split_low(dve, n.plus(14 + LEAD))
                add_out(dve, o, 2, 1)
            wait(dve, ydiag_done, g.times(2), 1)
            nc.vector.tensor_tensor(yn[:, 0, :], bank[4][:, :], dx[:, 0, :], ALU.add).then_inc(y_read, 1)
            seg(g, 3)
            weighted(g, 3)
            if not first:
                split_low(dve, n.plus(15 + LEAD))
                add_out(dve, o, 3, 0)
            wait(dve, nat_ready, g.times(2), 2)
            nc.vector.scalar_tensor_tensor(natz[:, :, :].rearrange("p t n -> p (t n)"),
                                           tz[:, :, :].rearrange("p t n -> p (t n)"), 1.0,
                                           natz[:, :, :].rearrange("p t n -> p (t n)"), ALU.add, ALU.mult)
            wait(dve, ydiag_done, g.times(2), 2)
            nc.vector.tensor_tensor(yn[:, 1, :], bank[5][:, :], dx[:, 1, :], ALU.add).then_inc(y_read, 1)
            wait(dve, yoff_done, g, 1)
            nc.vector.tensor_tensor(by_head(xdte[:, :]), by_head(bank[4][:, :]), wide(heads(ea[:, 1, :], g)),
                                    ALU.mult).then_inc(y_read, 1)
            dve.drain()
            nc.vector.tensor_tensor(yn[:, 1, :], yn[:, 1, :], xdte[:, :], ALU.add)
            dve.drain()
            nc.vector.tensor_tensor(yn[:, :, :], yn[:, :, :], natz[:, :, :], ALU.mult).then_inc(gated, 1)
            wait(dve, squared, g, 1)
            nc.vector.tensor_scalar(powin[:, 0:TT], ss[:, :], 1.0 / (4 * N), RMS_EPS, ALU.mult,
                                    ALU.add).then_inc(pow_asked, 1)
            wait(dve, pow_done, g, 1)
            for tt in range(TT):
                ins = nc.vector.tensor_scalar(yn[:, tt, :], yn[:, tt, :], powout[:, tt:tt + 1], 0.5, ALU.mult, ALU.mult)
            ins.then_inc(normed, 1)

        group(At(0), At(0), True)
        with dve.Fori(1, SSD_GROUPS) as it:
            group(At(0, 1, it), At(-4, 16, it), False)
        low_out(At(SSD_GROUPS - 1))
        last_out(dve, FOX_SLOT - 4)
        asked["pow"] += SSD_GROUPS

    def ssd_pool(pool):
        power(pool, At(1))
        with pool.Fori(1, SSD_GROUPS) as it:
            power(pool, At(1, 1, it))
        served_pool[0] += SSD_GROUPS


    MLA_HEAD, MIX_HEAD, CROSS_HEAD = 16, 32, 48
    V_AT = {"fox": 256, "mla": 320, "diff": 256, "flat": 256}
    WIDTH = {"fox": 512, "mla": 448, "diff": 384, "flat": 384}
    K_AT = {"fox": 128, "mla": 192, "diff": 128, "flat": 128}
    SCALE = {"fox": 128.0 ** -0.5, "mla": 192.0 ** -0.5, "diff": 64.0 ** -0.5, "flat": 128.0 ** -0.5}
    LAM_KEEP = 1.0 - (0.8 - 0.6)

    def pick(at):
        return slice(at.first, at.first + 1) if at.it is None else bass.ds(at.value(), 1)


    def turn_qk(pe, m, p, kind):
        wait(pe, head_nat, m, 1)
        wait(pe, qkT_ready, m)
        if kind == "mla":
            wait(pe, rope_ready, m, 2 - MLA_HEAD)
            wait(pe, probT_ready, m)
        for j, at in enumerate((0, K_AT[kind])):
            for tt in range(TT):
                ins = nc.tensor.transpose(bank[4][:, j * T + tt * P:j * T + tt * P + P],
                                          nat[:, p, tt, at:at + P], ident)
        if kind == "mla":
            for tt in range(TT):
                ins = nc.tensor.transpose(bank[6][0:64, tt * P:tt * P + P], qpe[:, tt, :], ident)
        ins.then_inc(qkT_done, 1)

    def scores(pe, m, kind):
        wait(pe, qkT_ready, m, 1)
        wait(pe, logits_ready, m)
        if kind == "diff":
            wait(pe, probT_ready, m)
        for c in range(2 if kind == "diff" else 1):
            rows = slice(64 * c, 64 * c + 64) if kind == "diff" else slice(0, P)
            for q, lo, keys in ((0, 0, P), (1, P, T)):
                at = slice(q * P, q * P + P)
                out = bank[5 + c][:, lo:lo + keys]
                ins = nc.tensor.matmul(out, qk[rows, 0, at], qk[rows, 1, 0:keys], start=True, stop=kind != "mla")
                if kind == "mla":
                    ins = nc.tensor.matmul(out, qpeT[:, at], kpeT[:, 0:keys], start=False, stop=True)
        ins.then_inc(scores_done, 1)

    def turn_probs(pe, m, kind):
        if kind == "diff":
            wait(pe, mixed_ready, m, 1 - MIX_HEAD)
        else:
            wait(pe, probs_ready, m, 1)
        wait(pe, probT_ready, m)
        for j in range(3):
            ins = nc.tensor.transpose(bank[6][:, j * P:j * P + P], prob[:, j * P:j * P + P], ident)
        ins.then_inc(probT_done, 1)

    def values(pe, m, p, kind):
        wait(pe, probT_ready, m, 1)
        wait(pe, headl_ready, m)
        v = [nat[:, p, tt, V_AT[kind]:V_AT[kind] + P] for tt in range(TT)]
        nc.tensor.matmul(bank[7][:, 0:P], probT[:, 0:P], v[0], start=True, stop=True)
        nc.tensor.matmul(bank[7][:, P:T], probT[:, P:2 * P], v[0], start=True, stop=False)
        nc.tensor.matmul(bank[7][:, P:T], probT[:, 2 * P:3 * P], v[1], start=False, stop=True).then_inc(pv_done, 1)

    def turn_head(pe, m):
        wait(pe, head_ready, m, 1)
        for tt in range(TT):
            ins = nc.tensor.transpose(bank[7][:, T + tt * P:T + tt * P + P], yh[:, tt, :], ident)
        ins.then_inc(headT_done, 1)


    def head_to_sbuf(act, m, p, pair, n, kind):
        wait(act, slots_used, n, 1)
        wait(act, head_ready, m, -1)
        for tt in range(TT):
            ins = nc.scalar.activation(nat[:, p, tt, 0:WIDTH[kind]], pairs[pair][tt][:, 0:WIDTH[kind]], ACT.Copy)
        ins.then_inc(free[pair], 1)
        act.drain()
        if kind == "fox":
            nc.scalar.activation(tzh[:, p, :, :], nat[:, p, :, 384:512], ACT.Tanh, scale=0.5).then_inc(head_nat, 1)
        else:
            act.drain().then_inc(head_nat, 1)

    def exponentials(act, m, kind):
        wait(act, logits_ready, m, 1)
        wait(act, probT_done, m)
        for c in range(2 if kind == "diff" else 1):
            for q, lo, keys in ((0, 0, P), (1, P, T)):
                nc.scalar.activation((prob, prob2)[c][:, lo:lo + keys], (logit, logit2)[c][:, lo:lo + keys], ACT.Exp,
                                     bias=nmax[:, c, q:q + 1], accum_out=psum_[:, c, q:q + 1])
        act.drain().then_inc(probs_ready, 1)

    def head_high(act, m, place, kind):
        wait(act, headT_done, m, 1)
        nc.scalar.activation(YH[:, place, :], bank[7][:, T:2 * T], ACT.Copy,
                             scale=subg[:, 0:1] if kind == "diff" else HEAD_SCALE[kind]).then_inc(headh_ready, 1)


    HEAD_SCALE = {"fox": 0.5, "mla": 0.5, "flat": 1.0}

    def qk_to_sbuf(dve, m, kind):
        wait(dve, scores_done, m)
        wait(dve, qkT_done, m, 1)
        if kind == "mla":
            nc.vector.tensor_copy(qpeT[:, :], bank[6][0:64, 0:T])
        nc.vector.tensor_copy(qk[:, :, :].rearrange("p j t -> p (j t)"), bank[4][:, :]).then_inc(qkT_ready, 1)

    def logits(dve, m, kind):
        if kind == "fox":
            dve.drain()
            for q, lo, keys in ((0, 0, P), (1, P, T)):
                nc.vector.scalar_tensor_tensor(
                    bias[:, lo:lo + keys], mask[:, lo:lo + keys], cumq[:, q, pick(m)],
                    cumk[:, pick(m), 0:keys].rearrange("p h t -> p (h t)"), ALU.add, ALU.subtract)
            dve.drain()
            added = bias[:, :]
        elif kind == "mla":
            added = mask
        else:
            added = toep[:, pick(m.plus(-MIX_HEAD)), :].rearrange("p h t -> p (h t)")
            if kind == "diff" and m.it is None:
                dve.wait_ge(toep_loaded, 16 * 2 * P // COPIES)
        if kind != "fox":
            dve.drain()
        wait(dve, probs_ready, m)
        wait(dve, scores_done, m, 1)
        for c in range(2 if kind == "diff" else 1):
            nc.vector.scalar_tensor_tensor((logit, logit2)[c][:, :], bank[5 + c][:, 0:384], SCALE[kind], added,
                                           ALU.mult, ALU.add)
        dve.drain()
        for c in range(2 if kind == "diff" else 1):
            for q, lo, keys in ((0, 0, P), (1, P, T)):
                ins = nc.vector.tensor_reduce(nmax[:, c, q:q + 1], (logit, logit2)[c][:, lo:lo + keys], axis=AX.X,
                                              op=ALU.max, negate=True)
        ins.then_inc(logits_ready, 1)

    def mix_maps(dve, m):
        wait(dve, probs_ready, m, 1)
        nc.vector.reciprocal(rsum[:, :, :].rearrange("p c q -> p (c q)"), psum_[:, :, :].rearrange("p c q -> p (c q)"))
        dve.drain()
        nc.vector.tensor_scalar(rsum[:, 1, :], rsum[:, 1, :], lam[:, 0:1], None, ALU.mult)
        dve.drain()
        for q, lo, keys in ((0, 0, P), (1, P, T)):
            nc.vector.tensor_scalar(prob2[:, lo:lo + keys], prob2[:, lo:lo + keys], rsum[:, 1, q:q + 1], None, ALU.mult)
        dve.drain()
        for q, lo, keys in ((0, 0, P), (1, P, T)):
            ins = nc.vector.scalar_tensor_tensor(prob[:, lo:lo + keys], prob[:, lo:lo + keys], rsum[:, 0, q:q + 1],
                                                 prob2[:, lo:lo + keys], ALU.mult, ALU.subtract)
        ins.then_inc(mixed_ready, 1)

    def probs_to_sbuf(dve, m, kind):
        dve.drain()
        wait(dve, pv_done, m)
        wait(dve, probT_done, m, 1)
        if kind != "diff":
            nc.vector.reciprocal(rsum[:, 0, :], psum_[:, 0, :])
        nc.vector.tensor_copy(probT[:, 0:384], bank[6][:, 0:384]).then_inc(probT_ready, 1)

    def head_output(dve, m, p, kind, place):
        if kind == "fox":
            nc.vector.scalar_tensor_tensor(zz[:, :, :], tzh[:, p, :, :], 1.0, nat[:, p, :, 384:512], ALU.add, ALU.mult)
        dve.drain()
        wait(dve, headT_done, m)
        wait(dve, pv_done, m, 1)
        for tt in range(TT):
            at = bank[7][:, tt * P:tt * P + P]
            if kind == "diff":
                ins = nc.vector.tensor_copy(yh[:, tt, :], at)
            elif kind == "flat":
                ins = nc.vector.tensor_scalar(yh[:, tt, :], at, rsum[:, 0, tt:tt + 1], None, ALU.mult)
            else:
                gate = zz[:, tt, :] if kind == "fox" else z4[:, tt, place * P:place * P + P]
                ins = nc.vector.scalar_tensor_tensor(yh[:, tt, :], at, rsum[:, 0, tt:tt + 1], gate, ALU.mult, ALU.mult)
        if kind != "diff":
            ins.then_inc(head_ready, 1)
            return
        dve.drain()
        nc.vector.tensor_tensor(zz[:, :, :], yh[:, :, :], yh[:, :, :], ALU.mult)
        dve.drain()
        nc.vector.tensor_reduce(ay[:, :], zz[:, :, :], axis=AX.X, op=ALU.add)
        dve.drain()
        nc.vector.tensor_scalar(powin[:, 0:TT], ay[:, :], 1.0 / P, RMS_EPS, ALU.mult, ALU.add).then_inc(pow_asked, 1)
        wait(dve, pow_done, m, 1 - MIX_HEAD + POWERS_BEFORE_MIX)
        for tt in range(TT):
            ins = nc.vector.tensor_scalar(yh[:, tt, :], yh[:, tt, :], powout[:, tt:tt + 1], None, ALU.mult)
        ins.then_inc(head_ready, 1)

    def head_low(dve, m, place, kind):
        wait(dve, headh_ready, m, 1)
        nc.vector.scalar_tensor_tensor(YL[:, place, :], bank[7][:, T:2 * T],
                                       subg[:, 0:1] if kind == "diff" else HEAD_SCALE[kind],
                                       YH[:, place, :].bitcast(F32), ALU.mult, ALU.subtract).then_inc(headl_ready, 1)


    def fox_tensor(pe, claims):
        pe.wait_ge(xl_ready, 16)
        pe.wait_ge(small_loaded, 32)
        small_products(pe, bank[4], 16).then_inc(pe_done, 1)
        served_pe[0] += 1
        pe.wait_ge(pe_asked, served_pe[0])
        nc.tensor.matmul(bank[5][:, 0:16], tri, lf[:, 0, :], start=True, stop=True)
        nc.tensor.matmul(bank[5][:, 16:32], ones, lf[:, 0, :], start=True, stop=False)
        nc.tensor.matmul(bank[5][:, 16:32], tri, lf[:, 1, :], start=False, stop=True).then_inc(pe_done, 1)
        for h in range(FOX_HEADS):
            b = bank[4 + (2 + h // 2) % 4]
            if h % 2 == 0 and h >= 4:
                pe.wait_ge(cum_read, max(h // 2 - 3, 1))
            lo = (h % 2) * T
            both = [lf[:, tt, h:h + 1].to_broadcast([P, P]) for tt in range(TT)]
            nc.tensor.matmul(b[:, lo:lo + P], both[0], tri, start=True, stop=True)
            nc.tensor.matmul(b[:, lo + P:lo + T], both[0], ones, start=True, stop=False)
            ins = nc.tensor.matmul(b[:, lo + P:lo + T], both[1], tri, start=False, stop=True)
            if h % 2:
                ins.then_inc(pe_done, 1)

        def body(m, n, first):
            o = 0
            for h in range(4):
                pair, p = h % 2, h % 2
                before, two = not (first and h == 0), not (first and h < 2)
                wait(pe, free[pair], claims.claim(pair))
                for s in range(4):
                    products(pe, n.plus(4 * h + s + o), 4, N, pair, s == 0, s == 3, k0=4 * s)
                    if s == 0 and two:
                        turn_head(pe, m.plus(h - 2))
                    if s == 0 and before:
                        turn_qk(pe, m.plus(h - 1), 1 - p, "fox")
                    if s == 1 and before:
                        scores(pe, m.plus(h - 1), "fox")
                    if s == 2 and before:
                        turn_probs(pe, m.plus(h - 1), "fox")
                    if s == 3 and before:
                        values(pe, m.plus(h - 1), 1 - p, "fox")
                if h == 1 and not first:
                    o = 4
                    wait(pe, headl_ready, m)
                    for c in range(4):
                        out_products_of(pe, claims, n.plus(8), c, c % 2)

        body(At(0), At(FOX_SLOT), True)
        with pe.Fori(1, 4) as it:
            claims.loop(it, (4, 4))
            body(At(0, 4, it), At(FOX_SLOT - 4, 20, it), False)
            claims.end(3)
        last_heads_tensor(pe, claims, FOX_HEADS - 1, "fox", MLA_SLOT - 4)

    def last_heads_tensor(pe, claims, m, kind, slot, chunks=4):
        turn_head(pe, At(m - 1))
        turn_qk(pe, At(m), m % 2, kind)
        scores(pe, At(m), kind)
        turn_probs(pe, At(m), kind)
        values(pe, At(m), m % 2, kind)
        turn_head(pe, At(m))
        pe.wait_ge(headl_ready, m + 1)
        for c in range(4):
            out_products_of(pe, claims, At(slot), c, c % 2, chunks)

    def last_heads_scalar(act, m, kind, slot, places=4):
        place = m % places
        head_high(act, At(m - 1), (m - 1) % places, kind)
        exponentials(act, At(m), kind)
        head_high(act, At(m), place, kind)
        for c in range(4):
            split_high(act, At(slot + c + LEAD))

    def last_heads_vector(dve, m, kind, slot, places=4):
        place = m % places
        head_low(dve, At(m - 1), (m - 1) % places, kind)
        if kind == "mla":
            dve.wait_ge(head_nat, m + 1)
            rotate(nat[:, m % 2, :, :], 128, qpe).then_inc(rope_ready, 1)
        qk_to_sbuf(dve, At(m), kind)
        logits(dve, At(m), kind)
        probs_to_sbuf(dve, At(m), kind)
        head_output(dve, At(m), m % 2, kind, place)
        head_low(dve, At(m), place, kind)
        last_out(dve, slot)

    def fox_scalar(act):
        served_act[0] += 1
        act.wait_ge(act_asked, served_act[0])
        nc.scalar.activation(f2[:, :, :], f2[:, :, :], ACT.Exp, scale=-1.0)
        act.drain()
        nc.scalar.activation(f3[:, :, :], f2[:, :, :], ACT.Ln, bias=1.0).then_inc(act_done, 1)

        def body(m, n, first):
            o = 0
            for h in range(4):
                p = h % 2
                before, two = not (first and h == 0), not (first and h < 2)
                for s in range(4):
                    split_high(act, n.plus(4 * h + s + o + LEAD))
                    if s == 0 and two:
                        head_high(act, m.plus(h - 2), (h - 2) % 4, "fox")
                    if s == 1 and before:
                        exponentials(act, m.plus(h - 1), "fox")
                head_to_sbuf(act, m.plus(h), p, p, n.plus(4 * h + 3 + o), "fox")
                if h == 1 and not first:
                    o = 4
                    for c in range(4):
                        split_high(act, n.plus(8 + c + LEAD))

        body(At(0), At(FOX_SLOT), True)
        with act.Fori(1, 4) as it:
            body(At(0, 4, it), At(FOX_SLOT - 4, 20, it), False)
        last_heads_scalar(act, FOX_HEADS - 1, "fox", MLA_SLOT - 4)

    def fox_vector(dve):
        dve.wait_ge(params_loaded, 16 * 5)
        dve.wait_ge(pe_done, 3)
        for tt in range(TT):
            nc.vector.tensor_tensor(f1[:, tt, :], bank[4][:, tt * 16:tt * 16 + 16], frow[:, :], ALU.add)
        dve.drain()
        nc.vector.scalar_tensor_tensor(f2[:, :, :], f1[:, :, :], -1.0, f1[:, :, :], ALU.mult, ALU.max).then_inc(act_asked, 1)
        dve.wait_ge(act_done, ask("act"))
        nc.vector.tensor_scalar(lf[:, :, :], f2[:, :, :], 1.0, None, ALU.add)
        dve.drain()
        nc.vector.reciprocal(cumq[:, :, :], lf[:, :, :])
        nc.vector.scalar_tensor_tensor(lf[:, :, :], lf[:, :, :], -1.0, f2[:, :, :], ALU.add, ALU.subtract)
        dve.drain()
        nc.vector.tensor_tensor(lf[:, :, :], lf[:, :, :], cumq[:, :, :], ALU.mult)
        dve.drain()
        nc.vector.tensor_tensor(f3[:, :, :], f3[:, :, :], lf[:, :, :], ALU.subtract)
        dve.drain()
        nc.vector.scalar_tensor_tensor(lf[:, :, :], f1[:, :, :], 0.0, f3[:, :, :], ALU.min, ALU.subtract).then_inc(pe_asked, 1)
        ask("pe")
        dve.wait_ge(pe_done, 4)
        nc.vector.tensor_copy(cumq[:, :, :].rearrange("p t h -> p (t h)"), bank[5][:, 0:32])
        for j in range(FOX_HEADS // 2):
            dve.wait_ge(pe_done, 5 + j)
            nc.vector.tensor_copy(cumk[:, 2 * j:2 * j + 2, :].rearrange("p h t -> p (h t)"),
                                  bank[4 + (2 + j) % 4][:, :]).then_inc(cum_read, 1)

        def body(m, n, first):
            o = 0
            for h in range(4):
                p = h % 2
                before, two = not (first and h == 0), not (first and h < 2)
                for s in range(4):
                    split_low(dve, n.plus(4 * h + s + o + LEAD))
                    if s == 0 and two:
                        head_low(dve, m.plus(h - 2), (h - 2) % 4, "fox")
                    if s == 0 and before:
                        qk_to_sbuf(dve, m.plus(h - 1), "fox")
                    if s == 1 and before:
                        logits(dve, m.plus(h - 1), "fox")
                    if s == 2 and before:
                        probs_to_sbuf(dve, m.plus(h - 1), "fox")
                    if s == 3 and before:
                        head_output(dve, m.plus(h - 1), 1 - p, "fox", None)
                if h == 1 and not first:
                    o = 4
                    for c in range(4):
                        split_low(dve, n.plus(8 + c + LEAD))
                        add_out(dve, n.plus(8), c, c % 2)

        body(At(0), At(FOX_SLOT), True)
        with dve.Fori(1, 4) as it:
            body(At(0, 4, it), At(FOX_SLOT - 4, 20, it), False)
        last_heads_vector(dve, FOX_HEADS - 1, "fox", MLA_SLOT - 4)


    MAGIC = 1.5 * 2.0 ** 23
    PI_1, PI_2, PI_3 = 6.28125, 0.0019350051879882812, 3.0199159819e-07
    PI_SAFE = 3.1415925

    def mla_tensor(pe, claims):
        pe.wait_ge(xl_ready, 24)
        for j in range(2):
            wait(pe, free[j], claims.claim(j))
            for s in range(4):
                products(pe, At(MLA_SLOT + 4 * j + s), 4, N, j, s == 0, s == 3, k0=4 * s)
        pe.wait_ge(small_loaded, 48)
        small_products(pe, bank[4], 64).then_inc(pe_done, 1)
        served_pe[0] += 1
        pe.wait_ge(pe_asked, served_pe[0])
        for j in range(2):
            for tt in range(TT):
                for k in range(4):
                    ins = nc.tensor.transpose(bank[4 + 2 * j + tt][:, k * P:k * P + P],
                                              lat[:, j, tt, k * P:k * P + P], ident)
                ins.then_inc(lat_done, 1)
        pe.wait_ge(latl_ready, 4)
        for tt in range(TT):
            ins = nc.tensor.transpose(bank[4][0:64, tt * P:tt * P + P], kper[:, tt, :], ident)
        ins.then_inc(pe_done, 1)
        pe.wait_ge(rope_ready, 1)

        def up(n, m, pair):
            wait(pe, free[pair], claims.claim(pair))
            products(pe, n, 4, 448, pair, True, True, LH, LL, cols=(0, 192), done=False)
            products(pe, n, 4, 448, pair, True, True, LH, LL, k0=4, cols=(192, 448))

        def body(m, n, first):
            o = n.plus(6 if first else 10)
            gate = [dict(k0=4 * s, only=part, done=part[-1] == 3) for s in range(3) for part in ((0, 1), (2, 3))]
            up(n, m, 0)
            if not first:
                scores(pe, m.plus(-2), "mla")
                turn_head(pe, m.plus(-3))
            wait(pe, free[1], claims.claim(1))
            products(pe, n.plus(1), 4, N, 1, True, False, **gate[0])
            if not first:
                turn_probs(pe, m.plus(-2), "mla")
            products(pe, n.plus(1), 4, N, 1, False, False, **gate[1])
            if not first:
                values(pe, m.plus(-2), 0, "mla")
            products(pe, n.plus(2), 4, N, 1, False, False, **gate[2])
            if not first:
                turn_qk(pe, m.plus(-1), 1, "mla")
            products(pe, n.plus(2), 4, N, 1, False, False, **gate[3])
            if not first:
                turn_head(pe, m.plus(-2))
                scores(pe, m.plus(-1), "mla")
            products(pe, n.plus(3), 4, N, 1, False, False, **gate[4])
            products(pe, n.plus(3), 4, N, 1, False, False, **gate[5])
            if not first:
                turn_probs(pe, m.plus(-1), "mla")
                values(pe, m.plus(-1), 1, "mla")
            up(n.plus(4), m, 0)
            if not first:
                turn_head(pe, m.plus(-1))
            turn_qk(pe, m, 0, "mla")
            products(pe, n.plus(5), 4, N, 1, False, True, k0=12)
            scores(pe, m, "mla")
            if not first:
                wait(pe, headl_ready, m)
                out_products_of(pe, claims, n.plus(6), 0, 0)
            turn_probs(pe, m, "mla")
            if not first:
                out_products_of(pe, claims, n.plus(6), 1, 1)
            values(pe, m, 0, "mla")
            turn_qk(pe, m.plus(1), 1, "mla")
            if not first:
                out_products_of(pe, claims, n.plus(6), 2, 0)
            scores(pe, m.plus(1), "mla")
            if not first:
                out_products_of(pe, claims, n.plus(6), 3, 1)
            turn_probs(pe, m.plus(1), "mla")
            up(o, m, 0)
            turn_head(pe, m)
            up(o.plus(1), m, 1)
            values(pe, m.plus(1), 1, "mla")
            turn_qk(pe, m.plus(2), 0, "mla")

        body(At(MLA_HEAD), At(MLA_SLOT + 8), True)
        with pe.Fori(1, 4) as it:
            claims.loop(it, (5, 4))
            body(At(MLA_HEAD, 4, it), At(MLA_SLOT + 4, 12, it), False)
            claims.end(3)
        m = At(MIX_HEAD - 2)
        scores(pe, m, "mla")
        turn_head(pe, m.plus(-1))
        turn_probs(pe, m, "mla")
        values(pe, m, 0, "mla")
        last_heads_tensor(pe, claims, MIX_HEAD - 1, "mla", S5_SLOT - 4)

    def mla_scalar(act):
        served_act[0] += 1
        act.wait_ge(act_asked, served_act[0])
        nc.scalar.activation(cossin[:, 1, :, :], ang[:, :, :], ACT.Sin)
        nc.scalar.activation(cossin[:, 0, :, :], ang[:, :, :], ACT.Sin, scale=0.5).then_inc(act_done, 1)
        for j in range(2):
            for s in range(4):
                split_high(act, At(MLA_SLOT + 4 * j + s + LEAD))
            evacuate(act, lat[:, j, :, :], j, At(MLA_SLOT + 4 * j + 3))
        act.drain()
        for j in range(2):
            for tt in range(TT):
                nc.scalar.activation(probT[:, :], lat[:, j, tt, :], ACT.Square, accum_out=psum_[:, j, tt:tt + 1])
                act.drain()
        act.drain().then_inc(nat_ready, 1)
        for j in range(2):
            for tt in range(TT):
                act.wait_ge(lat_done, 2 * j + tt + 1)
                nc.scalar.activation(LH[:, 4 * j:4 * j + 4, tt * P:tt * P + P],
                                     bank[4 + 2 * j + tt][:, :].rearrange("p (k t) -> p k t", k=4),
                                     ACT.Copy).then_inc(lath_ready, 1)

        def body(m, n, b, first):
            o = n.plus(6 if first else 10)
            split_high(act, n.plus(LEAD))
            if not first:
                head_high(act, m.plus(-3), 1, "mla")
                exponentials(act, m.plus(-2), "mla")
            split_high(act, n.plus(1 + LEAD))
            split_high(act, n.plus(2 + LEAD))
            head_to_sbuf(act, m, 0, 0, n, "mla")
            if not first:
                head_high(act, m.plus(-2), 2, "mla")
                exponentials(act, m.plus(-1), "mla")
            split_high(act, n.plus(3 + LEAD))
            split_high(act, n.plus(4 + LEAD))
            if not first:
                head_high(act, m.plus(-1), 3, "mla")
            head_to_sbuf(act, m.plus(1), 1, 0, n.plus(4), "mla")
            split_high(act, n.plus(5 + LEAD))
            wait(act, head_ready, m)
            evacuate(act, z4, 1, n.plus(5))
            exponentials(act, m, "mla")
            nc.scalar.activation(tz4, z4, ACT.Tanh, scale=0.5).then_inc(nat_ready, 1)
            if not first:
                for s in range(6, 10):
                    split_high(act, n.plus(s + LEAD))
            exponentials(act, m.plus(1), "mla")
            split_high(act, o.plus(LEAD))
            head_to_sbuf(act, m.plus(2), 0, 0, o, "mla")
            head_high(act, m, 0, "mla")
            split_high(act, o.plus(1 + LEAD))
            head_to_sbuf(act, m.plus(3), 1, 1, o.plus(1), "mla")

        body(At(MLA_HEAD), At(MLA_SLOT + 8), At(0), True)
        with act.Fori(1, 4) as it:
            body(At(MLA_HEAD, 4, it), At(MLA_SLOT + 4, 12, it), At(0, 1, it), False)
        head_high(act, At(MIX_HEAD - 3), 1, "mla")
        exponentials(act, At(MIX_HEAD - 2), "mla")
        last_heads_scalar(act, MIX_HEAD - 1, "mla", S5_SLOT - 4)

    def rotate(source, lo, target):
        x1, x2 = source[:, :, lo:lo + 32], source[:, :, lo + 32:lo + 64]
        cos, sin = cossin[:, 0, :, :], cossin[:, 1, :, :]
        nc.vector.tensor_tensor(rt[:, :, 0:32], x2, sin, ALU.mult)
        nc.vector.tensor_tensor(rt[:, :, 32:64], x1, sin, ALU.mult)
        nc.vector.tensor_tensor(target[:, :, 0:32], x1, cos, ALU.mult)
        nc.vector.tensor_tensor(target[:, :, 32:64], x2, cos, ALU.mult)
        nc.vector.drain()
        nc.vector.tensor_tensor(target[:, :, 0:32], target[:, :, 0:32], rt[:, :, 0:32], ALU.subtract)
        return nc.vector.tensor_tensor(target[:, :, 32:64], target[:, :, 32:64], rt[:, :, 32:64], ALU.add)

    def mla_vector(dve):
        dve.wait_ge(params_loaded, 16 * 7)
        nc.vector.tensor_copy(posf[:, :], angi[:, :])
        dve.drain()
        for tt in range(TT):
            nc.vector.tensor_scalar(ang[:, tt, :], con[:, C_FREQ:C_FREQ + 32], posf[:, tt:tt + 1], None, ALU.mult)
        dve.drain()
        whole_turns(dve, ang[:, :, :], angk[:, :, :]).then_inc(act_asked, 1)
        dve.wait_ge(act_done, ask("act"))
        nc.vector.tensor_tensor(angk[:, :, :], cossin[:, 0, :, :], cossin[:, 0, :, :], ALU.mult)
        dve.drain()
        nc.vector.tensor_scalar(cossin[:, 0, :, :], angk[:, :, :], -2.0, 1.0, ALU.mult, ALU.add)
        for s in range(8):
            split_low(dve, At(MLA_SLOT + s + LEAD))
        dve.wait_ge(pe_done, 13)
        nc.vector.tensor_copy(kpe[:, :, :].rearrange("p t c -> p (t c)"), bank[4][:, 0:128])
        dve.drain()
        rotate(kpe[:, :, :], 0, kper)
        dve.drain()
        dve.wait_ge(nat_ready, 17)
        nc.vector.tensor_scalar(powin[:, :], psum_[:, :, :].rearrange("p j t -> p (j t)"), 1.0 / N, RMS_EPS, ALU.mult,
                                ALU.add).then_inc(pow_asked, 1)
        dve.wait_ge(pow_done, ask("pow"))
        for j in range(2):
            for tt in range(TT):
                ins = nc.vector.scalar_tensor_tensor(lat[:, j, tt, :], lat[:, j, tt, :],
                                                     powout[:, 2 * j + tt:2 * j + tt + 1],
                                                     latw[:, j * N:j * N + N], ALU.mult, ALU.mult)
        ins.then_inc(pe_asked, 1)
        ask("pe")
        for j in range(2):
            for tt in range(TT):
                dve.wait_ge(lath_ready, 2 * j + tt + 1)
                at = (slice(None), slice(4 * j, 4 * j + 4), slice(tt * P, tt * P + P))
                nc.vector.tensor_tensor(LL[at], bank[4 + 2 * j + tt][:, :].rearrange("p (k t) -> p k t", k=4),
                                        LH[at].bitcast(F32), ALU.subtract).then_inc(latl_ready, 1)
        dve.wait_ge(pe_done, 14)
        nc.vector.tensor_copy(kpeT[:, :], bank[4][0:64, 0:T]).then_inc(rope_ready, 1)

        def turn_and_copy(m, p):
            wait(dve, head_nat, m, 1)
            wait(dve, qkT_done, m)
            rotate(nat[:, p, :, :], 128, qpe).then_inc(rope_ready, 1)
            qk_to_sbuf(dve, m, "mla")

        def body(m, n, b, first):
            o = n.plus(6 if first else 10)
            split_low(dve, n.plus(LEAD))
            if not first:
                logits(dve, m.plus(-2), "mla")
                head_low(dve, m.plus(-3), 1, "mla")
            split_low(dve, n.plus(1 + LEAD))
            if not first:
                probs_to_sbuf(dve, m.plus(-2), "mla")
                head_output(dve, m.plus(-2), 0, "mla", 2)
            split_low(dve, n.plus(2 + LEAD))
            if not first:
                turn_and_copy(m.plus(-1), 1)
                head_low(dve, m.plus(-2), 2, "mla")
                logits(dve, m.plus(-1), "mla")
            split_low(dve, n.plus(3 + LEAD))
            if not first:
                probs_to_sbuf(dve, m.plus(-1), "mla")
                head_output(dve, m.plus(-1), 1, "mla", 3)
            split_low(dve, n.plus(4 + LEAD))
            if not first:
                head_low(dve, m.plus(-1), 3, "mla")
            turn_and_copy(m, 0)
            split_low(dve, n.plus(5 + LEAD))
            logits(dve, m, "mla")
            wait(dve, nat_ready, b, 18)
            nc.vector.scalar_tensor_tensor(z4.rearrange("p t n -> p (t n)"), tz4.rearrange("p t n -> p (t n)"), 1.0,
                                           z4.rearrange("p t n -> p (t n)"), ALU.add, ALU.mult)
            if not first:
                split_low(dve, n.plus(6 + LEAD))
            probs_to_sbuf(dve, m, "mla")
            if not first:
                add_out(dve, n.plus(6), 0, 0)
                split_low(dve, n.plus(7 + LEAD))
            head_output(dve, m, 0, "mla", 0)
            if not first:
                add_out(dve, n.plus(6), 1, 1)
            turn_and_copy(m.plus(1), 1)
            if not first:
                split_low(dve, n.plus(8 + LEAD))
            logits(dve, m.plus(1), "mla")
            if not first:
                add_out(dve, n.plus(6), 2, 0)
                split_low(dve, n.plus(9 + LEAD))
            probs_to_sbuf(dve, m.plus(1), "mla")
            if not first:
                add_out(dve, n.plus(6), 3, 1)
            split_low(dve, o.plus(LEAD))
            head_low(dve, m, 0, "mla")
            split_low(dve, o.plus(1 + LEAD))
            head_output(dve, m.plus(1), 1, "mla", 1)
            turn_and_copy(m.plus(2), 0)

        body(At(MLA_HEAD), At(MLA_SLOT + 8), At(0), True)
        with dve.Fori(1, 4) as it:
            body(At(MLA_HEAD, 4, it), At(MLA_SLOT + 4, 12, it), At(0, 1, it), False)
        m = At(MIX_HEAD - 2)
        logits(dve, m, "mla")
        head_low(dve, m.plus(-1), 1, "mla")
        probs_to_sbuf(dve, m, "mla")
        head_output(dve, m, 0, "mla", 2)
        last_heads_vector(dve, MIX_HEAD - 1, "mla", S5_SLOT - 4)

    def whole_turns(dve, x, k):
        nc.vector.tensor_scalar(k, x, 1 / TWO_PI, MAGIC, ALU.mult, ALU.add)
        dve.drain()
        nc.vector.tensor_scalar(k, k, MAGIC, None, ALU.subtract)
        for part in (PI_1, PI_2, PI_3):
            dve.drain()
            nc.vector.scalar_tensor_tensor(x, k, -part, x, ALU.mult, ALU.add)
        dve.drain()
        return nc.vector.tensor_scalar(x, x, PI_SAFE, -PI_SAFE, ALU.min, ALU.max)


    LRE, LIM, LSTEP = 0, 1, 2
    RADIUS, THETA, TURN, SIN1, SINH, CRE, CIM, TMP = range(8)
    SCAN_TILES = 16
    TWO_PI_SAFE = 6.283185

    def s5_turns_pool(pool, i):
        wait(pool, part_ready, i)
        at = slice(2 * i.first, 2 * i.first + 2) if i.it is None else bass.ds(i.times(2).value(), 2)
        nc.gpsimd.tensor_tensor(turns5[:, :, :], iota.unsqueeze(1).to_broadcast([P, 2, T]),
                                co5[:, TURN, at].unsqueeze(2).to_broadcast([P, 2, T]), ALU.mult).then_inc(turns_ready, 1)

    def s5_part_vector(dve, i):
        wait(dve, turns_ready, i, 1)
        wait(dve, cs_ready, i)
        nc.vector.tensor_scalar(part5[:, :, :], turns5[:, :, :], MAGIC, None, ALU.add)
        dve.drain()
        nc.vector.scalar_tensor_tensor(part5[:, :, :], part5[:, :, :], MAGIC, turns5[:, :, :], ALU.subtract,
                                       ALU.subtract).then_inc(part_ready, 1)

    def s5_sin_scalar(act, i, buf, local):
        wait(act, part_ready, i, 1)
        if local > 0:
            wait(act, turned_back, i.times(2), -2)
        nc.scalar.activation(cs5[:, buf, 1, :, :], part5[:, :, :], ACT.Sin, scale=-TWO_PI_SAFE)
        nc.scalar.activation(cs5[:, buf, 0, :, :], part5[:, :, :], ACT.Abs)
        act.drain()
        nc.scalar.activation(cs5[:, buf, 0, :, :], cs5[:, buf, 0, :, :], ACT.Sin, scale=-TWO_PI_SAFE,
                             bias=halfpi[:, 0:1]).then_inc(cs_ready, 1)

    def s5_select_vector(dve, c, local):
        dve.drain()
        if local > 0:
            wait(dve, bcT_done, c)
        four = slice(0, 4) if c.it is None and c.first == 0 else (
            slice(4 * c.first, 4 * c.first + 4) if c.it is None else bass.ds(c.times(4).value(), 4))
        for half in range(2):
            nc.vector.tensor_scalar(bsel[:, :, :, 16 * half:16 * half + 16], b5[:, :, four, :],
                                    con[:, C_PAR + 2 + half:C_PAR + 3 + half], None, ALU.mult)
        for half in range(2):
            nc.vector.tensor_scalar(csel[:, 0, half:half + 1, :], c5[:, 0, pick(c), :],
                                    con[:, C_PAR + half:C_PAR + half + 1], None, ALU.mult)
            ins = nc.vector.tensor_scalar(csel[:, 1, half:half + 1, :], c5[:, 1, pick(c), :],
                                          con[:, C_PAR + half:C_PAR + half + 1], -1.0, ALU.mult, ALU.mult)
        ins.then_inc(sel_ready, 1)

    def s5_turn_bc(pe, c, local):
        wait(pe, sel_ready, c, 1)
        if local > 0:
            wait(pe, wc_ready, c)
        for x in range(2):
            nc.tensor.transpose(bank[6][:, x * P:x * P + P], bsel[:, x, :, :].rearrange("p j i -> p (j i)"), ident)
        for x in range(2):
            ins = nc.tensor.transpose(bank[6][:, (2 + x) * P:(3 + x) * P],
                                      csel[:, x, :, :].rearrange("p j i -> p (j i)"), ident)
        ins.then_inc(bcT_done, 1)

    def s5_tensor(pe, claims):
        pe.wait_ge(xl_ready, 32)

        def inputs_of(m, c, local):
            if local % 4 == 0:
                wait(pe, wb_ready, c, 1)
            if local >= 2:
                wait(pe, bu_read, m, -1)
            rows = slice(32 * (local % 4), 32 * (local % 4) + 32)
            b = bank[4 + local % 2]
            for x in range(2):
                ins = nc.tensor.matmul(b[:, x * T:x * T + T], wb5[rows, x, :],
                                       uchunk[rows, :], start=True, stop=True)
            ins.then_inc(bu_done, 1)

        def outputs_of(m, c, local):
            if local % 4 == 0:
                wait(pe, wc_ready, c, 1)
                if local:
                    wait(pe, y5_read, c)
            wait(pe, state_made, m, 1)
            at = P * (local % 4)
            for x in range(2):
                ins = nc.tensor.matmul(bank[7][:, 0:T], wc5[:, x * N + at:x * N + at + P], x5[:, local % 2, x, :],
                                       start=local % 4 == 0 and x == 0, stop=local % 4 == 3 and x == 1)
            ins.then_inc(y5_done, 1)

        def body(j, n, scan, slots=8):
            m, c = j.plus(-1).times(SCAN_TILES), j.plus(-1).times(4)
            for t in range(16):
                s = t // 2
                if slots:
                    if t % 8 == 0:
                        wait(pe, free[s // 4], claims.claim(s // 4))
                    products(pe, n.plus(s), 4, N, s // 4, s % 4 == 0, s % 4 == 3, k0=4 * (s % 4), done=t % 2,
                             only=(0, 1) if t % 2 == 0 else (2, 3))
                    if t == 11:
                        wait(pe, unat_ready, j, 1)
                        wait(pe, free[0], claims.claim(0))
                        for k in range(4):
                            for tt in range(TT):
                                ins = nc.tensor.transpose(
                                    bank[k // 2][:, (k % 2) * T + tt * P:(k % 2) * T + tt * P + P],
                                    unat[:, tt, k * P:k * P + P], ident)
                        ins.then_inc(uT_done, 1)
                if not scan:
                    continue
                if t == 0:
                    wait(pe, uT_ready, j)
                    s5_turn_bc(pe, c, 0)
                inputs_of(m.plus(t), c.plus(t // 4), t)
                if t % 4 == 3 and t < 15:
                    s5_turn_bc(pe, c.plus(t // 4 + 1), t // 4 + 1)
                if t >= 3:
                    outputs_of(m.plus(t - 3), c.plus((t - 3) // 4), t - 3)
            if scan:
                for t in (13, 14, 15):
                    outputs_of(m.plus(t), c.plus(t // 4), t)

        body(At(0), At(S5_SLOT), False)
        with pe.Fori(1, 4) as it:
            claims.loop(it, (2, 1))
            body(At(0, 1, it), At(S5_SLOT, 8, it), True)
            claims.end(3)
        body(At(4), None, True, 0)

        def glu(j, n, first):
            wait(pe, free[1], claims.claim(1))
            for s in range(4):
                if first:
                    pe.wait_ge(y5l_ready, s + 1)
                products(pe, n.plus(s), 4, N, 1, s == 0, s == 3, k0=4 * s)
            if not first:
                wait(pe, o5l_ready, j)
                for c in range(2):
                    out_products_of(pe, claims, n.plus(4), c, c % 2)
            wait(pe, glu_nat, j, 1)
            wait(pe, zgate_ready, j, 1)
            wait(pe, glu_read, j)
            for source, b in ((w5[:, 0, :, :].rearrange("p (t k) n -> p t (k n)", t=TT), 4),
                              (z5[:, :, bass.ds(j.times(N).value(), N)], 6)):
                for k in range(4):
                    for tt in range(TT):
                        ins = nc.tensor.transpose(
                            bank[b + k // 2][:, (k % 2) * T + tt * P:(k % 2) * T + tt * P + P],
                            w5[:, 1, :, :].rearrange("p (t k) n -> p t (k n)", t=TT)[:, tt, k * P:k * P + P]
                            if b == 6 else source[:, tt, k * P:k * P + P], ident)
            ins.then_inc(gluT_done, 1)
            if not first:
                for c in range(2, 4):
                    out_products_of(pe, claims, n.plus(4), c, c % 2)

        glu(At(0), At(S5_SLOT + 32), True)
        with pe.Fori(1, 4) as it:
            claims.loop(it, (2, 3))
            glu(At(0, 1, it), At(S5_SLOT + 28, 8, it), False)
            claims.end(3)
        pe.wait_ge(o5l_ready, 4)
        for c in range(4):
            out_products_of(pe, claims, At(CKV_SLOT - 4), c, c % 2)

    def s5_scalar(act):
        def reply():
            served_act[0] += 1
            act.wait_ge(act_asked, served_act[0])

        reply()
        nc.scalar.activation(co5[:, TMP, :], par5[:, LSTEP, :], ACT.Exp).then_inc(act_done, 1)
        split_high(act, At(S5_SLOT + LEAD))
        reply()
        nc.scalar.activation(co5[:, RADIUS, :], co5[:, RADIUS, :], ACT.Exp)
        nc.scalar.activation(co5[:, SIN1, :], co5[:, THETA, :], ACT.Sin)
        nc.scalar.activation(co5[:, SINH, :], co5[:, THETA, :], ACT.Sin, scale=0.5).then_inc(act_done, 1)

        def body(j, n, scan, slots=8, last=False):
            m, c, i = j.plus(-1).times(SCAN_TILES), j.plus(-1).times(4), j.plus(-1).times(8)
            for s in range(8):
                if slots:
                    if not (s == 0 and not scan):
                        split_high(act, n.plus(s + LEAD))
                    if s == 4:
                        wait(act, uT_done, j)
                        evacuate(act, unat, 0, n.plus(3))
                        act.drain().then_inc(unat_ready, 1)
                    if s == 6:
                        wait(act, uT_done, j, 1)
                        for b in range(2):
                            lo = j.times(4).plus(2 * b)
                            at = slice(lo.first, lo.first + 2) if lo.it is None else bass.ds(lo.value(), 2)
                            ins = nc.scalar.activation(u5[:, at, :], bank[b][:, :].rearrange("p (k t) -> p k t", k=2),
                                                       ACT.Copy)
                        ins.then_inc(free[0], 1)
                        act.drain().then_inc(uT_ready, 1)
                if not scan:
                    continue
                cl = s // 2
                if s % 2 == 0:
                    cc = c.plus(cl)
                    wait(act, bcT_done, cc, 1)
                    nc.scalar.activation(uchunk, u5[:, pick(cc), :].rearrange("p c t -> p (c t)"), ACT.Copy)
                    nc.scalar.activation(wb5[:, :, :].rearrange("p x i -> p (x i)"), bank[6][:, 0:T],
                                         ACT.Copy).then_inc(wb_ready, 1)
                if slots or s < 7:
                    s5_sin_scalar(act, i.plus(s + 1), (s + 1) % 2, s)
                if s % 2 == 0:
                    if cl:
                        wait(act, y5_done, m.plus(4 * cl))
                    for x in range(2):
                        ins = nc.scalar.activation(
                            wc5[:, x * N:x * N + 640].rearrange("p (j w) -> p j w", w=160)[:, :, 0:32],
                            bank[6][:, (2 + x) * P:(3 + x) * P].rearrange("p (j w) -> p j w", j=4), ACT.Copy)
                    ins.then_inc(wc_ready, 1)
            if slots:
                if not scan:
                    act.wait_ge(b5_ready, 1)
                    s5_sin_scalar(act, At(0), 0, 0)
                wait(act, slots_used, n, 8)
                for tt in range(TT):
                    if last:
                        at = unat[:, tt, :]
                    else:
                        at = z5[:, tt, bass.ds(j.times(N).value(), N) if j.it is not None else slice(0, N)]
                    ins = nc.scalar.activation(at, bank[2 + tt][:, :], ACT.Copy)
                ins.then_inc(free[1], 1)

        body(At(0), At(S5_SLOT), False)
        with act.Fori(1, 3) as it:
            body(At(0, 1, it), At(S5_SLOT, 8, it), True)
        body(At(3), At(S5_SLOT + 24), True, last=True)
        body(At(4), None, True, 0, True)
        act.wait_ge(y5_done, 64)
        nc.scalar.activation(z5[:, :, 3 * N:4 * N], unat, ACT.Copy)
        for q in range(4):
            act.wait_ge(y5_read, min(4 * q + 4, 16))
            at = u5[:, 4 * q:4 * q + 4, :]
            nc.scalar.activation(at, at, ACT.Gelu_apprx_tanh)
            act.drain()
            nc.scalar.activation(XH[:, 4 * q:4 * q + 4, :], at, ACT.Copy).then_inc(y5h_ready, 1)

        def glu(j, n, first):
            for s in range(4):
                split_high(act, n.plus(s + LEAD))
            wait(act, gluT_done, j)
            nat_z = w5[:, 1, :, :].rearrange("p (t k) n -> p t (k n)", t=TT)
            at = bass.ds(j.times(N).value(), N) if j.it is not None else slice(0, N)
            nc.scalar.activation(nat_z, z5[:, :, at], ACT.Tanh, scale=0.5).then_inc(ztanh_ready, 1)
            evacuate(act, w5[:, 0, :, :].rearrange("p (t k) n -> p t (k n)", t=TT), 1, n.plus(3))
            act.drain().then_inc(glu_nat, 1)
            if not first:
                for s in range(4, 6):
                    split_high(act, n.plus(s + LEAD))
            wait(act, gluT_done, j, 1)
            wait(act, o5l_ready, j)
            for k in range(4):
                kk = j.times(4).plus(k)
                ins = nc.scalar.activation(q5[:, k, :], bank[4 + k // 2][:, (k % 2) * T:(k % 2) * T + T], ACT.Tanh,
                                           scale=0.5, bias=bg5[:, pick(kk)])
            ins.then_inc(gtanh5_ready, 1)
            if not first:
                for s in range(6, 8):
                    split_high(act, n.plus(s + LEAD))
                wait(act, slots_used, n, 8)
            wait(act, o5_ready, j, 1)
            nc.scalar.activation(YH[:, :, :], q5[:, :, :], ACT.Copy).then_inc(o5h_ready, 1)

        glu(At(0), At(S5_SLOT + 32), True)
        with act.Fori(1, 4) as it:
            glu(At(0, 1, it), At(S5_SLOT + 28, 8, it), False)
        for c in range(2):
            split_high(act, At(CKV_SLOT - 4 + c + LEAD))
        turn_scalar(act, 4)
        for c in range(2, 4):
            split_high(act, At(CKV_SLOT - 4 + c + LEAD))

    def s5_vector(dve):
        dve.wait_ge(s5_loaded, 80)
        dve.drain().then_inc(act_asked, 1)
        dve.wait_ge(act_done, ask("act"))
        nc.vector.tensor_tensor(co5[:, RADIUS, :], par5[:, LRE, :], co5[:, TMP, :], ALU.mult)
        nc.vector.tensor_tensor(co5[:, THETA, :], par5[:, LIM, :], co5[:, TMP, :], ALU.mult)
        nc.vector.tensor_scalar(bg5[:, :], bg5[:, :], 0.5, None, ALU.mult)
        dve.drain()
        whole_turns(dve, co5[:, THETA, :], co5[:, CRE, :])
        dve.drain()
        nc.vector.tensor_scalar(co5[:, TURN, :], co5[:, THETA, :], 1 / TWO_PI, None, ALU.mult).then_inc(act_asked, 1)
        split_low(dve, At(S5_SLOT + LEAD))
        dve.wait_ge(act_done, ask("act"))
        nc.vector.tensor_tensor(co5[:, SIN1, :], co5[:, SIN1, :], co5[:, RADIUS, :], ALU.mult)
        nc.vector.tensor_tensor(co5[:, SINH, :], co5[:, SINH, :], co5[:, SINH, :], ALU.mult)
        dve.drain()
        nc.vector.scalar_tensor_tensor(co5[:, SINH, :], co5[:, SINH, :], -2.0, co5[:, RADIUS, :], ALU.mult, ALU.mult)
        dve.drain()
        nc.vector.scalar_tensor_tensor(co5[:, SINH, :], co5[:, RADIUS, :], -1.0, co5[:, SINH, :], ALU.add, ALU.add)
        nc.vector.tensor_tensor(co5[:, TMP, :], par5[:, LRE, :], par5[:, LRE, :], ALU.mult)
        nc.vector.tensor_tensor(co5[:, THETA, :], par5[:, LIM, :], par5[:, LIM, :], ALU.mult)
        dve.drain()
        nc.vector.tensor_tensor(co5[:, TMP, :], co5[:, TMP, :], co5[:, THETA, :], ALU.add)
        dve.drain()
        nc.vector.reciprocal(co5[:, TMP, :], co5[:, TMP, :])
        nc.vector.tensor_tensor(co5[:, CRE, :], co5[:, SINH, :], par5[:, LRE, :], ALU.mult)
        nc.vector.tensor_tensor(co5[:, CIM, :], co5[:, SIN1, :], par5[:, LRE, :], ALU.mult)
        nc.vector.tensor_tensor(co5[:, SIN1, :], co5[:, SIN1, :], par5[:, LIM, :], ALU.mult)
        nc.vector.tensor_tensor(co5[:, SINH, :], co5[:, SINH, :], par5[:, LIM, :], ALU.mult)
        dve.drain()
        nc.vector.tensor_tensor(co5[:, CRE, :], co5[:, CRE, :], co5[:, SIN1, :], ALU.add)
        nc.vector.tensor_tensor(co5[:, CIM, :], co5[:, CIM, :], co5[:, SINH, :], ALU.subtract)
        dve.drain()
        nc.vector.tensor_tensor(co5[:, CRE, :], co5[:, CRE, :], co5[:, TMP, :], ALU.mult)
        nc.vector.tensor_tensor(co5[:, CIM, :], co5[:, CIM, :], co5[:, TMP, :], ALU.mult).then_inc(co5_ready, 1)

        def scan(m, local):
            b = local % 2
            cos, sin = (cs5[:, (local // 2) % 2, x, b:b + 1, :].to_broadcast([P, 2, T]) for x in range(2))
            if local % 2 == 0:
                wait(dve, cs_ready, m.half(), 1)
            if local >= 2:
                wait(dve, turned_back, m, -1)
            wait(dve, bu_done, m, 1)
            bu = bank[4 + b][:, :].rearrange("p (x t) -> p x t", x=2)
            nc.vector.tensor_tensor(w5[:, b, 0:2, :], bu, cos, ALU.mult)
            nc.vector.tensor_tensor(w5[:, b, 2:4, :], bu, sin, ALU.mult).then_inc(bu_read, 1)
            dve.drain()
            nc.vector.tensor_tensor(w5[:, b, 0, :], w5[:, b, 0, :], w5[:, b, 3, :], ALU.add)
            nc.vector.tensor_tensor(w5[:, b, 1, :], w5[:, b, 1, :], w5[:, b, 2, :], ALU.subtract)
            dve.drain()
            radius = co5[:, RADIUS, pick(m)].to_broadcast([P, T])
            for x in range(2):
                ins = nc.vector.tensor_tensor_scan(w5[:, b, 2 + x, :], radius, w5[:, b, x, :], 0.0, ALU.mult, ALU.add)
            ins.then_inc(scanned, 1)

        def output(c):
            wait(dve, y5_done, c.times(4), 4)
            at = u5[:, pick(c), :].rearrange("p c t -> p (c t)")
            nc.vector.scalar_tensor_tensor(at, at, d5[:, pick(c)], bank[7][:, 0:T], ALU.mult, ALU.add).then_inc(y5_read, 1)

        def body(j, n, scanning, slots=8, last=False):
            m, c, i = j.plus(-1).times(SCAN_TILES), j.plus(-1).times(4), j.plus(-1).times(8)
            if scanning:
                s5_select_vector(dve, c, 0)
            for s in range(8):
                if slots and not (s == 0 and not scanning):
                    split_low(dve, n.plus(s + LEAD))
                if not scanning:
                    continue
                if not (last and s == 7):
                    s5_part_vector(dve, i.plus(s + 1))
                for t in (2 * s, 2 * s + 1):
                    if t % 4 == 3 and t > 3:
                        output(c.plus(t // 4 - 1))
                    scan(m.plus(t), t)
                    if t % 4 == 0 and t < 12:
                        s5_select_vector(dve, c.plus(t // 4 + 1), t // 4 + 1)
            if scanning:
                output(c.plus(3))

        body(At(0), At(S5_SLOT), False)
        s5_part_vector(dve, At(0))
        dve.wait_ge(b5_ready, 1)
        with dve.Fori(1, 4) as it:
            body(At(0, 1, it), At(S5_SLOT, 8, it), True)
        body(At(4), None, True, 0, True)
        for q in range(4):
            dve.wait_ge(y5h_ready, q + 1)
            at = (slice(None), slice(4 * q, 4 * q + 4), slice(None))
            nc.vector.tensor_tensor(XL[at], u5[at], XH[at].bitcast(F32), ALU.subtract).then_inc(y5l_ready, 1)

        def glu(j, n, first):
            for s in range(4):
                split_low(dve, n.plus(s + LEAD))
            wait(dve, ztanh_ready, j, 1)
            nat_z = w5[:, 1, :, :].rearrange("p (t k) n -> p t (k n)", t=TT)
            at = bass.ds(j.times(N).value(), N) if j.it is not None else slice(0, N)
            nc.vector.scalar_tensor_tensor(nat_z, nat_z, 1.0, z5[:, :, at], ALU.add, ALU.mult).then_inc(zgate_ready, 1)
            if not first:
                for c in range(2):
                    split_low(dve, n.plus(4 + c + LEAD))
                    add_out(dve, n.plus(4), c, c % 2)
            wait(dve, gtanh5_ready, j, 1)
            at = j.times(4)
            at = slice(0, 4) if at.it is None else bass.ds(at.value(), 4)
            nc.vector.scalar_tensor_tensor(q5[:, :, :], q5[:, :, :], 1.0, u5[:, at, :], ALU.add, ALU.mult)
            dve.drain()
            for b in range(2):
                ins = nc.vector.scalar_tensor_tensor(q5[:, 2 * b:2 * b + 2, :],
                                                     bank[6 + b][:, :].rearrange("p (k t) -> p k t", k=2), 0.25,
                                                     q5[:, 2 * b:2 * b + 2, :], ALU.mult, ALU.mult)
            ins.then_inc(o5_ready, 1)
            dve.drain().then_inc(glu_read, 1)
            if not first:
                for c in range(2, 4):
                    split_low(dve, n.plus(4 + c + LEAD))
                    add_out(dve, n.plus(4), c, c % 2)
            wait(dve, o5h_ready, j, 1)
            nc.vector.tensor_tensor(YL[:, :, :], q5[:, :, :], YH[:, :, :].bitcast(F32), ALU.subtract).then_inc(o5l_ready, 1)

        glu(At(0), At(S5_SLOT + 32), True)
        with dve.Fori(1, 4) as it:
            glu(At(0, 1, it), At(S5_SLOT + 28, 8, it), False)
        slot = CKV_SLOT - 4
        for c in range(2):
            split_low(dve, At(slot + c + LEAD))
            add_out(dve, At(slot), c, c % 2)
        dve.wait_ge(mem_loaded, 16)
        for k in range(4):
            statistics(dve, src, k)
        rms_norm_vector(dve, 4, src, src)
        for c in range(2, 4):
            add_out(dve, At(slot), c, c % 2)
        turn_vector(dve, 4)
        for c in range(2, 4):
            split_low(dve, At(slot + c + LEAD))
        for k in range(4):
            statistics(dve, acc, k)

    def s5_pool(pool):
        pool.wait_ge(src_ready, 12)
        pool.dma_start(par5[:, :, :], a["s5_par"]).then_inc(s5_loaded, 16)
        pool.dma_start(gain[:, :], a["s5_b"]).then_inc(s5_loaded, 16)
        pool.dma_start(offs[:, :], a["s5_c"]).then_inc(s5_loaded, 16)
        pool.dma_start(d5[:, :], a["s5_d"]).then_inc(s5_loaded, 16)
        pool.dma_start(bg5[:, :], a["s5_bglu"]).then_inc(s5_loaded, 16)
        nc.gpsimd.memset(wc5[:, :], 0.0)
        nc.gpsimd.memset(halfpi[:, :], np.pi / 2)
        pool.wait_ge(s5_loaded, 80)
        pool.wait_ge(co5_ready, 1)
        z = z5[:, :, :].rearrange("p a (b t i) -> p (a b) t i", b=2, i=16)
        for i, (x, y) in enumerate(((CRE, 0), (CIM, 1), (CRE, 1), (CIM, 0))):
            nc.gpsimd.tensor_tensor(z[:, i, :, :], b5[:, y, :, :], co5[:, x, :].unsqueeze(2).to_broadcast([P, 64, 16]),
                                    ALU.mult)
        pool.drain()
        nc.gpsimd.tensor_tensor(b5[:, 0, :, :], z[:, 0, :, :], z[:, 1, :, :], ALU.subtract)
        nc.gpsimd.tensor_tensor(b5[:, 1, :, :], z[:, 2, :, :], z[:, 3, :, :], ALU.add).then_inc(b5_ready, 1)
        s5_turns_pool(pool, At(0))
        s5_turns_pool(pool, At(1))

        def body(j, last=False):
            m, i = j.plus(-1).times(SCAN_TILES), j.plus(-1).times(8)
            for t in range(16):
                if t % 2 and not (last and t > 11):
                    s5_turns_pool(pool, i.plus((t + 1) // 2 + 1))
                b = t % 2
                cos, sin = (cs5[:, (t // 2) % 2, x, b:b + 1, :].to_broadcast([P, 2, T]) for x in range(2))
                wait(pool, scanned, m.plus(t), 1)
                nc.gpsimd.tensor_tensor(q5[:, 0:2, :], w5[:, b, 2:4, :], cos, ALU.mult)
                nc.gpsimd.tensor_tensor(q5[:, 2:4, :], w5[:, b, 2:4, :], sin, ALU.mult).then_inc(turned_back, 1)
                pool.drain()
                if t >= 2:
                    wait(pool, y5_done, m.plus(t), -1)
                nc.gpsimd.tensor_tensor(x5[:, b, 0, :], q5[:, 0, :], q5[:, 3, :], ALU.subtract)
                nc.gpsimd.tensor_tensor(x5[:, b, 1, :], q5[:, 1, :], q5[:, 2, :], ALU.add).then_inc(state_made, 1)
                pool.drain()

        with pool.Fori(1, 4) as it:
            body(At(0, 1, it))
        body(At(4), True)


    POWERS_BEFORE_MIX = SSD_GROUPS + 3 + 1 + 3

    def memory_tensor(pe, claims):
        pe.wait_ge(xl_ready, 40)
        for j in range(2):
            wait(pe, free[j], claims.claim(j))
            for s in range(4):
                products(pe, At(CKV_SLOT + 4 * j + s), 4, N, j, s == 0, s == 3, k0=4 * s)
                if (j, s) == (1, 1):
                    pe.wait_ge(mix_loaded, 80)
                    nc.tensor.matmul(bank[7][0:16, :], rtab[:, :], rhot[:, :], start=True,
                                     stop=True).then_inc(bias_done, 1)
                if (j, s) == (1, 2):
                    pe.wait_ge(kv_nat, 1)
                    for h in range(MEM_HEADS):
                        for tt in range(TT):
                            ins = nc.tensor.transpose(
                                bank[4 + h // 2][:, (h % 2) * T + tt * P:(h % 2) * T + tt * P + P],
                                knat[:, tt, h * P:h * P + P], ident)
                    ins.then_inc(kT_done, 1)
        pe.wait_ge(kT_ready, 1)
        pe.wait_ge(rvec_ready, 1)

    def memory_scalar(act):
        for s in range(4):
            split_high(act, At(CKV_SLOT + s + LEAD))
        evacuate(act, knat, 0, At(CKV_SLOT + 3))
        act.drain().then_inc(kv_nat, 1)
        for s in range(4, 6):
            split_high(act, At(CKV_SLOT + s + LEAD))
        served_act[0] += 1
        act.wait_ge(act_asked, served_act[0])
        nc.scalar.activation(lam[:, 2:4], lam[:, 2:4], ACT.Exp).then_inc(act_done, 1)
        split_high(act, At(CKV_SLOT + 6 + LEAD))
        act.wait_ge(kT_done, 1)
        for b in range(2):
            nc.scalar.activation(memk[:, 2 * b:2 * b + 2, :].rearrange("p h t -> p (h t)"), bank[4 + b][:, :], ACT.Copy)
        act.drain().then_inc(kT_ready, 1)
        split_high(act, At(CKV_SLOT + 7 + LEAD))
        evacuate(act, memv, 1, At(CKV_SLOT + 7))

    def memory_vector(dve):
        split_low(dve, At(CKV_SLOT + LEAD))
        layer_norm_vector(dve, 5)
        for s in range(1, 4):
            split_low(dve, At(CKV_SLOT + s + LEAD))
        for c in range(4):
            statistics(dve, acc, c)
        split_low(dve, At(CKV_SLOT + 4 + LEAD))
        rms_norm_vector(dve, 6, acc, src)
        split_low(dve, At(CKV_SLOT + 5 + LEAD))
        dve.wait_ge(mix_loaded, 80)
        nc.vector.tensor_tensor(lprod[:, :, :], lrow[:, 0:4:2, :], lrow[:, 1:4:2, :], ALU.mult)
        nc.vector.tensor_scalar(subg[:, :], subg[:, :], LAM_KEEP, None, ALU.mult)
        dve.drain()
        nc.vector.tensor_reduce(lam[:, 2:4], lprod[:, :, :], axis=AX.X, op=ALU.add).then_inc(act_asked, 1)
        dve.wait_ge(act_done, ask("act"))
        nc.vector.scalar_tensor_tensor(lam[:, 0:1], lam[:, 2:3], 1.0 - LAM_KEEP, lam[:, 3:4], ALU.add, ALU.subtract)
        dve.wait_ge(bias_done, 1)
        nc.vector.tensor_tensor(rvec[:, :], bank[7][0:16, :], radd[:, :], ALU.add).then_inc(rvec_ready, 1)
        for s in range(6, 8):
            split_low(dve, At(CKV_SLOT + s + LEAD))

    def memory_pool(pool):
        pool.wait_ge(glu_read, 4)
        pool.dma_start(src[:, :, :], a["mem"].rearrange("(t p) d -> p t d", p=P)).then_inc(mem_loaded, 16)
        served_pool[0] += 1
        power(pool, served_pool[0])
        load_norm(pool, 5)
        served_pool[0] += 1
        power(pool, served_pool[0])
        load_norm(pool, 6)
        pool.dma_start(rtab[:, :], a["table"]).then_inc(mix_loaded, 16)
        pool.dma_start(rhot[:, :], a["hot"]).then_inc(mix_loaded, 16)
        pool.dma_start(radd[:, :], a["add"]).then_inc(mix_loaded, 16)
        pool.dma_start(lrow[:, :, :], a["lambda"].rearrange("o r n -> (o r) n").partition_broadcast(P)).then_inc(mix_loaded, 16)
        pool.dma_start(subg[:, :], a["subln"]).then_inc(mix_loaded, 16)
        served_pool[0] += 1
        power(pool, served_pool[0])
        load_norm(pool, 7)
        pool.wait_ge(rvec_ready, 1)
        pool.dma_start(rvec_dram.rearrange("p h i -> h p i"),
                       rvec[:, :].unsqueeze(1).to_broadcast([MIX_HEADS, COPIES, N])).then_inc(rvec_stored, 16)
        pool.wait_ge(rvec_stored, 16)
        for q in range(0, P, COPIES):
            for lo, keys, first in ((0, P, 255), (P, T, 127)):
                rows = bass.AP(rvec_dram.tensor, first - q, [[MIX_HEADS * N - 1, COPIES], [N, MIX_HEADS], [1, keys]])
                pool.dma_start(toep[q:q + COPIES, :, lo:lo + keys], rows).then_inc(toep_loaded, 16)


    def mix_tensor(pe, claims):
        pe.wait_ge(xl_ready, 48)

        def body(m, n, kind, before, first):
            for h in range(2):
                wait(pe, free[h], claims.claim(h))
                one, two = not (first and h == 0), not first
                was = kind if h else before
                for s in range(4):
                    for part in ((0, 1), (2, 3)) if s == 0 else (range(4),):
                        products(pe, n.plus(4 * h + s), 4, 384, h, s == 0, s == 3, k0=4 * s, done=part[-1] == 3,
                                 only=part)
                        if part[-1] == 1 and one:
                            turn_qk(pe, m.plus(h - 1), 1 - h, was)
                    if s == 0 and one:
                        scores(pe, m.plus(h - 1), was)
                    if s == 1 and two:
                        turn_head(pe, m.plus(h - 2))
                    if s == 2 and one:
                        turn_probs(pe, m.plus(h - 1), was)
                    if s == 3 and one:
                        values(pe, m.plus(h - 1), 1 - h, was)
            if not first:
                wait(pe, headl_ready, m)
                for c in range(4):
                    out_products_of(pe, claims, n.plus(8), c, c % 2, 2)

        def loop(lo, hi, kind):
            with pe.Fori(lo, hi) as it:
                claims.loop(it, (3, 3), lo)
                body(At(MIX_HEAD, 2, it), At(MIX_SLOT - 4, 12, it), kind, kind, False)
                claims.end(hi - lo)

        body(At(MIX_HEAD), At(MIX_SLOT), "diff", "diff", True)
        loop(1, 3, "diff")
        body(At(MIX_HEAD + 6), At(MIX_SLOT + 32), "flat", "diff", False)
        loop(4, 8, "flat")
        last_heads_tensor(pe, claims, CROSS_HEAD - 1, "flat", CROSS_SLOT - 4, 2)

    def mix_scalar(act):
        def body(m, n, kind, before, first):
            for h in range(2):
                was = kind if h else before
                for s in range(4):
                    split_high(act, n.plus(4 * h + s + LEAD))
                    if s == 1 and not (first and h == 0):
                        exponentials(act, m.plus(h - 1), was)
                    if s == 1 and not first:
                        head_high(act, m.plus(h - 2), h, before)
                head_to_sbuf(act, m.plus(h), h, h, n.plus(4 * h + 3), kind)
            if not first:
                for c in range(4):
                    split_high(act, n.plus(8 + c + LEAD))

        body(At(MIX_HEAD), At(MIX_SLOT), "diff", "diff", True)
        with act.Fori(1, 3) as it:
            body(At(MIX_HEAD, 2, it), At(MIX_SLOT - 4, 12, it), "diff", "diff", False)
        body(At(MIX_HEAD + 6), At(MIX_SLOT + 32), "flat", "diff", False)
        with act.Fori(4, 8) as it:
            body(At(MIX_HEAD, 2, it), At(MIX_SLOT - 4, 12, it), "flat", "flat", False)
        last_heads_scalar(act, CROSS_HEAD - 1, "flat", CROSS_SLOT - 4, 2)

    def mix_vector(dve):
        def body(m, n, kind, before, first):
            for h in range(2):
                was = kind if h else before
                one = not (first and h == 0)
                for s in range(4):
                    split_low(dve, n.plus(4 * h + s + LEAD))
                    if s == 0 and one:
                        qk_to_sbuf(dve, m.plus(h - 1), was)
                        logits(dve, m.plus(h - 1), was)
                    if s == 1 and not first:
                        head_low(dve, m.plus(h - 2), h, before)
                    if s == 2 and one:
                        if was == "diff":
                            mix_maps(dve, m.plus(h - 1))
                        probs_to_sbuf(dve, m.plus(h - 1), was)
                    if s == 3 and one:
                        head_output(dve, m.plus(h - 1), 1 - h, was, None)
            if not first:
                for c in range(4):
                    split_low(dve, n.plus(8 + c + LEAD))
                    add_out(dve, n.plus(8), c, c % 2)

        body(At(MIX_HEAD), At(MIX_SLOT), "diff", "diff", True)
        with dve.Fori(1, 3) as it:
            body(At(MIX_HEAD, 2, it), At(MIX_SLOT - 4, 12, it), "diff", "diff", False)
        body(At(MIX_HEAD + 6), At(MIX_SLOT + 32), "flat", "diff", False)
        with dve.Fori(4, 8) as it:
            body(At(MIX_HEAD, 2, it), At(MIX_SLOT - 4, 12, it), "flat", "flat", False)
        last_heads_vector(dve, CROSS_HEAD - 1, "flat", CROSS_SLOT - 4, 2)
        asked["pow"] += 6

    def mix_pool(pool):
        with pool.Fori(1, 7) as it:
            power(pool, At(POWERS_BEFORE_MIX, 1, it))
        served_pool[0] += 6


    CROSS_BANKS = (6, 7, 4, 5)
    HEADS = range(MEM_HEADS)

    def cross_tensor(pe, claims):
        pe.wait_ge(xl_ready, 56)
        wait(pe, free[0], claims.claim(0))
        for s in range(4):
            products(pe, At(CROSS_SLOT + s), 4, N, 0, s == 0, s == 3, k0=4 * s)
        pe.wait_ge(cq_nat, 1)
        for h in HEADS:
            for tt in range(TT):
                ins = nc.tensor.transpose(bank[4 + h // 2][:, (h % 2) * T + tt * P:(h % 2) * T + tt * P + P],
                                          nat[:, 0, tt, h * P:h * P + P], ident)
        ins.then_inc(cqT_done, 1)
        qT = nat[:, 1, :, :].rearrange("p t (h n) -> p (t h) n", n=T)
        pe.wait_ge(cqT_ready, 1)
        for h in HEADS:
            for tt in range(TT):
                ins = nc.tensor.matmul(bank[CROSS_BANKS[h]][:, tt * T:tt * T + T], qT[:, h, tt * P:tt * P + P],
                                       memk[:, h, :], start=True, stop=True)
            ins.then_inc(cs_done, 1)
        for h in HEADS:
            pe.wait_ge(cprob_ready, h + 1)
            for kc in range(TT):
                for tt in range(TT):
                    ins = nc.tensor.transpose(bank[CROSS_BANKS[h]][:, kc * T + tt * P:kc * T + tt * P + P],
                                              cprob[:, h, tt, kc * P:kc * P + P], ident)
            ins.then_inc(cpT_done, 1)
        wait(pe, free[1], claims.claim(1))
        for h in HEADS:
            pe.wait_ge(cpT_ready, h + 1)
            for tt in range(TT):
                for kc in range(TT):
                    ins = nc.tensor.matmul(pairs[1][tt][:, h * P:h * P + P],
                                           cprobT[:, h, kc * T + tt * P:kc * T + tt * P + P],
                                           memv[:, kc, h * P:h * P + P], start=kc == 0, stop=kc == 1)
        ins.then_inc(cpv_done, 1)
        pe.wait_ge(co_nat, 1)
        for h in HEADS:
            for tt in range(TT):
                ins = nc.tensor.transpose(bank[4 + h // 2][:, (h % 2) * T + tt * P:(h % 2) * T + tt * P + P],
                                          nat[:, 0, tt, h * P:h * P + P], ident)
        ins.then_inc(coT_done, 1)
        pe.wait_ge(col_ready, 1)
        for c in range(4):
            out_products_of(pe, claims, At(CROSS_SLOT + 4), c, c % 2)

    def cross_scalar(act):
        for s in range(4):
            split_high(act, At(CROSS_SLOT + s + LEAD))
        evacuate(act, nat[:, 0, :, :], 0, At(CROSS_SLOT + 3))
        act.drain().then_inc(cq_nat, 1)
        for h in HEADS:
            act.wait_ge(cmax_ready, h + 1)
            for tt in range(TT):
                ins = nc.scalar.activation(cprob[:, h, tt, :], bank[CROSS_BANKS[h]][:, tt * T:tt * T + T], ACT.Exp,
                                           scale=SCALE["flat"], bias=cmax[:, h, tt:tt + 1],
                                           accum_out=csum[:, h, tt:tt + 1])
            act.drain().then_inc(cprob_ready, 1)
        act.wait_ge(coT_done, 1)
        for b in range(2):
            nc.scalar.activation(YH[:, 2 * b:2 * b + 2, :].rearrange("p h t -> p (h t)"), bank[4 + b][:, :], ACT.Copy)
        act.drain().then_inc(coh_ready, 1)
        for s in range(4, 8):
            split_high(act, At(CROSS_SLOT + s + LEAD))

    def cross_vector(dve):
        for s in range(4):
            split_low(dve, At(CROSS_SLOT + s + LEAD))
        dve.wait_ge(cqT_done, 1)
        qT = nat[:, 1, :, :].rearrange("p t (h n) -> p (t h n)", n=T)
        for b in range(2):
            ins = nc.vector.tensor_copy(qT[:, b * N:b * N + N], bank[4 + b][:, :])
        dve.drain().then_inc(cqT_ready, 1)
        for h in HEADS:
            dve.wait_ge(cs_done, h + 1)
            nc.vector.tensor_reduce(cmax[:, h, :], bank[CROSS_BANKS[h]][:, :].rearrange("p (t k) -> p t k", t=TT),
                                    axis=AX.X, op=ALU.max, negate=True)
            dve.drain()
            nc.vector.tensor_scalar(cmax[:, h, :], cmax[:, h, :], SCALE["flat"], None, ALU.mult).then_inc(cmax_ready, 1)
        for h in HEADS:
            dve.wait_ge(cpT_done, h + 1)
            nc.vector.tensor_copy(cprobT[:, h, :], bank[CROSS_BANKS[h]][:, :]).then_inc(cpT_ready, 1)
        nc.vector.reciprocal(csum[:, :, :], csum[:, :, :])
        dve.drain()
        dve.wait_ge(cpv_done, 1)
        for tt in range(TT):
            ins = nc.vector.tensor_tensor(nat[:, 0, tt, :].rearrange("p (h n) -> p h n", n=P),
                                          pairs[1][tt][:, :].rearrange("p (h n) -> p h n", n=P),
                                          csum[:, :, tt:tt + 1].to_broadcast([P, MEM_HEADS, P]), ALU.mult)
        ins.then_inc(free[1], 1)
        dve.drain().then_inc(co_nat, 1)
        dve.wait_ge(coh_ready, 1)
        for b in range(2):
            nc.vector.tensor_tensor(YL[:, 2 * b:2 * b + 2, :].rearrange("p h t -> p (h t)"), bank[4 + b][:, :],
                                    YH[:, 2 * b:2 * b + 2, :].bitcast(F32).rearrange("p h t -> p (h t)"), ALU.subtract)
        dve.drain().then_inc(col_ready, 1)
        last_out(dve, CROSS_SLOT + 4)


    FF_BLOCKS = DFF // N

    def ffn_tensor(pe, claims):
        pe.wait_ge(xl_ready, 64)

        def turn_block(source, b):
            for k in range(4):
                for tt in range(TT):
                    ins = nc.tensor.transpose(bank[b + k // 2][:, (k % 2) * T + tt * P:(k % 2) * T + tt * P + P],
                                              source[:, tt, k * P:k * P + P], ident)
            return ins

        def turn_up(i):
            wait(pe, unat2_ready, i, 1)
            turn_block(natu, 6).then_inc(uT2_done, 1)

        def body(i, n, first):
            wait(pe, free[0], claims.claim(0))
            for s in range(4):
                products(pe, n.plus(s), 4, N, 0, s == 0, s == 3, k0=4 * s)
                if s == 0 and not first:
                    turn_up(i.plus(-1))
            u = n.plus(4)
            if not first:
                wait(pe, fl_ready, i)
                out_products_of(pe, claims, n.plus(4), 0, 1)
                u = n.plus(8)
            else:
                wait(pe, free[1], claims.claim(1))
                products(pe, u, 4, N, 1, True, False)
            wait(pe, gnat_ready, i, 1)
            wait(pe, gconv_ready, i)
            turn_block(natg, 4).then_inc(gT_done, 1)
            if not first:
                for c in range(1, 4):
                    out_products_of(pe, claims, n.plus(4), c, 1 - c % 2)
                wait(pe, free[1], claims.claim(1))
                products(pe, u, 4, N, 1, True, False)
            for s in range(1, 4):
                products(pe, u.plus(s), 4, N, 1, False, s == 3, k0=4 * s)

        body(At(0), At(FFN_SLOT), True)
        with pe.Fori(1, FF_BLOCKS) as it:
            claims.loop(it, (3, 3))
            body(At(0, 1, it), At(FFN_SLOT - 4, 12, it), False)
            claims.end(FF_BLOCKS - 1)
        turn_up(At(FF_BLOCKS - 1))
        pe.wait_ge(fl_ready, FF_BLOCKS)
        for c in range(4):
            out_products_of(pe, claims, At(SLOTS - 4), c, c % 2)

    def ffn_scalar(act):
        def high(i):
            wait(act, hidden_ready, i, 1)
            nc.scalar.activation(YH[:, :, :], hh[:, :, :], ACT.Copy).then_inc(fh_ready, 1)

        def body(i, n, first):
            for s in range(4):
                split_high(act, n.plus(s + LEAD))
                if s == 1 and not first:
                    high(i.plus(-1))
            wait(act, gT_done, i)
            evacuate(act, natg, 0, n.plus(3))
            act.drain().then_inc(gnat_ready, 1)
            u = n.plus(4) if first else n.plus(8)
            if not first:
                for s in range(4, 8):
                    split_high(act, n.plus(s + LEAD))
            split_high(act, u.plus(LEAD))
            wait(act, gconv_ready, i, 1)
            nc.scalar.activation(tg[:, :, :], gc[:, :, :], ACT.Tanh, scale=0.5).then_inc(gtanh_ready, 1)
            for s in range(1, 4):
                split_high(act, u.plus(s + LEAD))
            wait(act, uT2_done, i)
            evacuate(act, natu, 1, u.plus(3))
            act.drain().then_inc(unat2_ready, 1)

        body(At(0), At(FFN_SLOT), True)
        with act.Fori(1, FF_BLOCKS) as it:
            body(At(0, 1, it), At(FFN_SLOT - 4, 12, it), False)
        high(At(FF_BLOCKS - 1))
        for c in range(4):
            split_high(act, At(SLOTS - 4 + c + LEAD))

    def ffn_vector(dve):
        dve.wait_ge(fw_loaded, 16)

        def hidden(i):
            wait(dve, uT2_done, i, 1)
            for b in range(2):
                nc.vector.scalar_tensor_tensor(hh[:, 2 * b:2 * b + 2, :],
                                               bank[6 + b][:, :].rearrange("p (k t) -> p k t", k=2), 0.5,
                                               gc[:, 2 * b:2 * b + 2, :], ALU.mult, ALU.mult)
            dve.drain().then_inc(hidden_ready, 1)

        def low(i):
            wait(dve, fh_ready, i, 1)
            nc.vector.tensor_tensor(YL[:, :, :], hh[:, :, :], YH[:, :, :].bitcast(F32), ALU.subtract).then_inc(fl_ready, 1)

        def body(i, n, first):
            dve.drain()
            at = i.times(4)
            at = slice(0, 4) if at.it is None else bass.ds(at.value(), 4)
            nc.vector.tensor_copy(fwg[:, :, :], fw[:, :, at])
            for s in range(4):
                split_low(dve, n.plus(s + LEAD))
                if s == 0 and not first:
                    hidden(i.plus(-1))
                if s == 1 and not first:
                    low(i.plus(-1))
            u = n.plus(4) if first else n.plus(8)
            if not first:
                split_low(dve, n.plus(4 + LEAD))
                add_out(dve, n.plus(4), 0, 1)
            else:
                split_low(dve, u.plus(LEAD))
            wait(dve, gT_done, i, 1)
            for j in range(3):
                for k in range(4):
                    b = bank[4 + k // 2][:, (k % 2) * T:(k % 2) * T + T]
                    if j == 0:
                        nc.vector.tensor_scalar(gc[:, k, :], b, fwg[:, 2, k:k + 1], fwg[:, 3, k:k + 1], ALU.mult, ALU.add)
                    else:
                        nc.vector.scalar_tensor_tensor(gc[:, k, j:T], b[:, 0:T - j], fwg[:, 2 - j, k:k + 1],
                                                       gc[:, k, j:T], ALU.mult, ALU.add)
                if j < 2:
                    dve.drain()
            dve.drain().then_inc(gconv_ready, 1)
            if not first:
                for c in range(1, 4):
                    split_low(dve, n.plus(4 + c + LEAD))
                    add_out(dve, n.plus(4), c, 1 - c % 2)
                split_low(dve, u.plus(LEAD))
            wait(dve, gtanh_ready, i, 1)
            nc.vector.scalar_tensor_tensor(gc[:, :, :], tg[:, :, :], 1.0, gc[:, :, :], ALU.add, ALU.mult)
            for s in range(1, 4):
                split_low(dve, u.plus(s + LEAD))

        body(At(0), At(FFN_SLOT), True)
        with dve.Fori(1, FF_BLOCKS) as it:
            body(At(0, 1, it), At(FFN_SLOT - 4, 12, it), False)
        hidden(At(FF_BLOCKS - 1))
        low(At(FF_BLOCKS - 1))
        last_out(dve, SLOTS - 4)


    block = keep.enter_context(nc.Block())

    @block.sync
    def _(sp):
        sp.dma_start(acc[:, :, :], a["x"].rearrange("(t p) d -> p t d", p=P)).then_inc(x_loaded, 16)
        for s in range(RAWS):
            sp.dma_start(raw[:, s, :], a["stream"][s]).then_inc(raw_loaded[s], 16)
        with sp.Fori(1, SLOTS // RAWS) as it:
            for s in range(RAWS):
                sp.wait_ge(lo_ready, it * RAWS + (s + 1 - RAWS))
                sp.dma_start(raw[:, s, :], a["stream"][bass.ds(it * RAWS + s, 1), :, :].rearrange("s p n -> (s p) n")).then_inc(raw_loaded[s], 16)
        for tt in range(TT):
            sp.wait_ge(src_ready, 32 + 2 * tt + 2)
            sp.dma_start(a["y"][tt * P:tt * P + P, :], src[:, tt, :]).then_inc(out_stored, 16)
        sp.wait_ge(out_stored, 32)

    @block.gpsimd
    def _(pool):
        pool.dma_start(con[:, :], a["con"]).then_inc(params_loaded, 16)
        pool.dma_start(hrow[:, :, :], a["ssd_rows"].partition_broadcast(P)).then_inc(params_loaded, 16)
        pool.dma_start(cw[:, :, :], a["ssd_taps"]).then_inc(params_loaded, 16)
        pool.dma_start(nw[:, :], a["ssd_norm"]).then_inc(params_loaded, 16)
        pool.dma_start(small[:, :, :], a["ssd_dt"]).then_inc(small_loaded, 16)
        load_norm(pool, 1)
        pool.wait_ge(params_loaded, 64)
        ssd_pool(pool)
        pool.dma_start(frow[:, :], a["fox_bias"].rearrange("o h -> (o h)").partition_broadcast(P)).then_inc(params_loaded, 16)
        pool.dma_start(small[:, :, :], a["fox_f"]).then_inc(small_loaded, 16)
        power(pool, served_pool[0] + 1)
        served_pool[0] += 1
        load_norm(pool, 2)
        power(pool, served_pool[0] + 1)
        served_pool[0] += 1
        load_norm(pool, 3)
        pool.dma_start(angi[:, :], a["positions"]).then_inc(params_loaded, 16)
        pool.dma_start(latw[:, :], a["lat_w"].rearrange("o h -> (o h)").partition_broadcast(P)).then_inc(params_loaded, 16)
        pool.dma_start(small[:, :, :], a["mla_kpe"]).then_inc(small_loaded, 16)
        power(pool, served_pool[0] + 1, 4)
        served_pool[0] += 1
        power(pool, served_pool[0] + 1)
        served_pool[0] += 1
        s5_pool(pool)
        pool.wait_ge(sel_ready, 16)
        load_norm(pool, 4)
        memory_pool(pool)
        mix_pool(pool)
        served_pool[0] += 1
        power(pool, served_pool[0])
        load_norm(pool, 8)
        served_pool[0] += 1
        power(pool, served_pool[0])
        load_norm(pool, 9)
        pool.dma_start(fw[:, :, :], a["ff_taps"]).then_inc(fw_loaded, 16)
        served_pool[0] += 1
        power(pool, served_pool[0])

    @block.scalar
    def _(act):
        turn_scalar(act, 0)
        for n in range(LEAD):
            split_high(act, At(n))
        ssd_scalar(act)
        turn_scalar(act, 1)
        fox_scalar(act)
        turn_scalar(act, 2)
        mla_scalar(act)
        turn_scalar(act, 3)
        s5_scalar(act)
        memory_scalar(act)
        turn_scalar(act, 5)
        mix_scalar(act)
        turn_scalar(act, 6)
        cross_scalar(act)
        turn_scalar(act, 7)
        ffn_scalar(act)

    @block.vector
    def _(dve):
        turn_vector(dve, 0)
        for n in range(LEAD):
            split_low(dve, At(n))
        dve.wait_ge(xt_done, 8)
        scale_residual(dve)
        ssd_vector(dve)
        layer_norm_vector(dve, 1)
        turn_vector(dve, 1)
        dve.wait_ge(xt_done, 16)
        scale_residual(dve)
        fox_vector(dve)
        layer_norm_vector(dve, 2)
        turn_vector(dve, 2)
        dve.wait_ge(xt_done, 24)
        scale_residual(dve)
        mla_vector(dve)
        layer_norm_vector(dve, 3)
        turn_vector(dve, 3)
        dve.wait_ge(xt_done, 32)
        scale_residual(dve)
        s5_vector(dve)
        memory_vector(dve)
        turn_vector(dve, 5)
        mix_vector(dve)
        rms_norm_vector(dve, 7, acc, src)
        turn_vector(dve, 6)
        cross_vector(dve)
        rms_norm_vector(dve, 8, acc, src)
        turn_vector(dve, 7)
        ffn_vector(dve)
        rms_norm_vector(dve, 9, acc, src)

    @block.tensor
    def _(pe):
        claims = Claims()
        turn_tensor(pe, 0, acc)
        ssd_tensor(pe, claims)
        turn_tensor(pe, 1, acc)
        fox_tensor(pe, claims)
        turn_tensor(pe, 2, acc)
        mla_tensor(pe, claims)
        turn_tensor(pe, 3, acc)
        s5_tensor(pe, claims)
        pe.wait_ge(glu_read, 4)
        turn_tensor(pe, 4, src)
        memory_tensor(pe, claims)
        turn_tensor(pe, 5, src)
        mix_tensor(pe, claims)
        turn_tensor(pe, 6, src)
        cross_tensor(pe, claims)
        turn_tensor(pe, 7, src)
        ffn_tensor(pe, claims)


def kernel(**inputs):
    import concourse.bacc as bacc
    from concourse.bass_utils import run_bass_kernel_spmd

    nc = bacc.Bacc("TRN2", target_bir_lowering=False, num_devices=1, dynamic_dma_scratch_size=4096)
    data = arrays(inputs)
    ins = {f"in_{k}": np.ascontiguousarray(v) for k, v in data.items()}
    a = {k: nc.dram_tensor(f"in_{k}", v.shape, mybir.dt.from_np(v.dtype), kind="ExternalInput").ap()
         for k, v in data.items()}
    a["y"] = nc.dram_tensor("out_y", (T, D), F32, kind="ExternalOutput").ap()
    build(nc, a)
    result = run_bass_kernel_spmd(nc, [ins], core_ids=[0])
    return result.results[0]["out_y"].reshape(1, T, D)
```
